# Optimizing a Trainium2 kernel written in Bass

```python
import jax, jax.numpy as jnp
from jax import lax
import numpy as np
import math

D_MODEL = 1024
BATCH = 1
SEQ = 256
DEPTH = 2

CHUNK = 64
EPS = 1e-6
N_A = DEPTH // 2
N_B = DEPTH - N_A
A_CHUNK = 128
A_DFF = 2 * D_MODEL
A_GROUPS = 8
A_GROUP_DIM = A_DFF // A_GROUPS
B_HEADS = 16
B_HEAD_DIM = D_MODEL // B_HEADS
N_LEFT_CHUNKS = 8
BAND = (N_LEFT_CHUNKS + 1) * CHUNK
MAX_REL = 256
ATTN_SCALE = B_HEAD_DIM ** -0.5
NEG_INF = -1e30
FFN_HIDDEN = -(-8 * D_MODEL // (3 * 256)) * 256


def _rms_norm(x, g):
    xf = x.astype(jnp.float32)
    y = xf * lax.rsqrt(jnp.mean(xf * xf, axis=-1, keepdims=True) + EPS)
    return (y * g.astype(jnp.float32)).astype(x.dtype)

def _spatial_mask():
    pos = jnp.arange(A_CHUNK) // CHUNK
    return pos[:, None] >= pos[None, :]

def _gmlp_mixer(x, g_norm, w_in, g_sgu, w_s, b_s, w_out):
    b, s, _ = x.shape
    h = _rms_norm(x, g_norm)
    z = jax.nn.gelu(h @ w_in, approximate=False)
    u, v = jnp.split(z, 2, axis=-1)
    v = _rms_norm(v, g_sgu)
    v = v.reshape(b, s // A_CHUNK, A_CHUNK, A_GROUPS, A_GROUP_DIM)
    w = w_s * _spatial_mask().astype(w_s.dtype)[None]
    v = jnp.einsum('gij,bnjgc->bnigc', w, v) + b_s.T[None, None, :, :, None]
    v = v.reshape(b, s, A_DFF)
    return (u * v) @ w_out

def _swiglu_ffn(x, g_norm, w_gate_up, w_down):
    h = _rms_norm(x, g_norm)
    gate, up = jnp.split(h @ w_gate_up, 2, axis=-1)
    return (jax.nn.silu(gate) * up) @ w_down

def _shared_kv(x, g_norm, w_kv):
    b, s, _ = x.shape
    h = _rms_norm(x, g_norm)
    k, v = jnp.split(h @ w_kv, 2, axis=-1)
    k = k.reshape(b, s, B_HEADS, B_HEAD_DIM)
    v = v.reshape(b, s, B_HEADS, B_HEAD_DIM)
    pad = ((0, 0), (N_LEFT_CHUNKS * CHUNK, 0), (0, 0), (0, 0))
    return jnp.pad(k, pad), jnp.pad(v, pad)

def _rel_index():
    qi = jnp.arange(CHUNK)[:, None]
    kj = jnp.arange(BAND)[None, :] - N_LEFT_CHUNKS * CHUNK
    return jnp.clip(qi - kj, -MAX_REL, MAX_REL) + MAX_REL

def _chunked_relbias_attention(x, g_norm, w_q, rel_table, w_o, k_pad, v_pad):
    b, s, _ = x.shape
    n_chunks = s // CHUNK
    q = (_rms_norm(x, g_norm) @ w_q).reshape(b, n_chunks, CHUNK, B_HEADS, B_HEAD_DIM)
    q = jnp.moveaxis(q, 1, 0)
    bias = rel_table[:, _rel_index()].astype(jnp.float32)
    key_offset = jnp.arange(BAND) - N_LEFT_CHUNKS * CHUNK

    def attend(args):
        c, q_c = args
        k_c = lax.dynamic_slice_in_dim(k_pad, c * CHUNK, BAND, axis=1)
        v_c = lax.dynamic_slice_in_dim(v_pad, c * CHUNK, BAND, axis=1)
        sc = jnp.einsum('bqhd,bkhd->bhqk', q_c, k_c).astype(jnp.float32) * ATTN_SCALE + bias
        valid = (c * CHUNK + key_offset) >= 0
        sc = jnp.where(valid, sc, NEG_INF)
        p = jax.nn.softmax(sc, axis=-1).astype(v_c.dtype)
        return jnp.einsum('bhqk,bkhd->bqhd', p, v_c)

    o = lax.map(attend, (jnp.arange(n_chunks), q))
    o = jnp.moveaxis(o, 0, 1).reshape(b, s, D_MODEL)
    return o @ w_o

def _normal(key, shape, scale):
    return jax.random.normal(key, shape, jnp.float32) * scale

def first_inputs(seed: int = 0) -> dict:
    key = jax.random.key(seed)
    ks = jax.random.split(key, 18)
    return {
        "x": _normal(ks[0], (BATCH, SEQ, D_MODEL), 1.0),
        "a_norm": 1.0 + _normal(ks[1], (N_A, D_MODEL), 0.02),
        "a_w_in": _normal(ks[2], (N_A, D_MODEL, 2 * A_DFF), D_MODEL ** -0.5),
        "a_sgu_norm": 1.0 + _normal(ks[3], (N_A, A_DFF), 0.02),
        "a_w_spatial": _normal(ks[4], (N_A, A_GROUPS, A_CHUNK, A_CHUNK), A_CHUNK ** -0.5),
        "a_b_spatial": 1.0 + _normal(ks[5], (N_A, A_GROUPS, A_CHUNK), 0.1),
        "a_w_out": _normal(ks[6], (N_A, A_DFF, D_MODEL), A_DFF ** -0.5),
        "kv_norm": 1.0 + _normal(ks[7], (D_MODEL,), 0.02),
        "w_kv": _normal(ks[8], (D_MODEL, 2 * D_MODEL), D_MODEL ** -0.5),
        "b_norm": 1.0 + _normal(ks[9], (N_B, D_MODEL), 0.02),
        "b_w_q": _normal(ks[10], (N_B, D_MODEL, D_MODEL), D_MODEL ** -0.5),
        "b_rel_bias": _normal(ks[11], (N_B, B_HEADS, 2 * MAX_REL + 1), 0.1),
        "b_w_o": _normal(ks[12], (N_B, D_MODEL, D_MODEL), D_MODEL ** -0.5),
        "ffn_norm": 1.0 + _normal(ks[13], (DEPTH, D_MODEL), 0.02),
        "ffn_w_gate_up": _normal(ks[14], (DEPTH, D_MODEL, 2 * FFN_HIDDEN), D_MODEL ** -0.5),
        "ffn_w_down": _normal(ks[15], (DEPTH, FFN_HIDDEN, D_MODEL), FFN_HIDDEN ** -0.5),
        "final_norm": 1.0 + _normal(ks[16], (D_MODEL,), 0.02),
    }

def first_block(x, a_norm, a_w_in, a_sgu_norm, a_w_spatial, a_b_spatial, a_w_out,
              kv_norm, w_kv, b_norm, b_w_q, b_rel_bias, b_w_o,
              ffn_norm, ffn_w_gate_up, ffn_w_down, final_norm):
    k_pad = v_pad = None
    for layer in range(DEPTH):
        if layer < N_A:
            i = layer
            x = x + _gmlp_mixer(x, a_norm[i], a_w_in[i], a_sgu_norm[i],
                                a_w_spatial[i], a_b_spatial[i], a_w_out[i])
        else:
            if layer == N_A:
                k_pad, v_pad = _shared_kv(x, kv_norm, w_kv)
            i = layer - N_A
            x = x + _chunked_relbias_attention(x, b_norm[i], b_w_q[i], b_rel_bias[i],
                                               b_w_o[i], k_pad, v_pad)
        x = x + _swiglu_ffn(x, ffn_norm[layer], ffn_w_gate_up[layer], ffn_w_down[layer])
    return _rms_norm(x, final_norm)


CONV_CH = D_MODEL // 4
CONV_WIDTH = 31
MOBA_HEADS = 4
MOBA_HEAD_DIM = D_MODEL // 16
MOBA_WIDTH = MOBA_HEADS * MOBA_HEAD_DIM
MOBA_BLOCK = 256
MOBA_TOPK = 3
MOBA_Q_CHUNK = 64
GLA_HEADS = 4
GLA_WIDTH = D_MODEL // 2
GLA_DV = GLA_WIDTH // GLA_HEADS
GLA_DK = GLA_DV // 2
GLA_GATE_RANK = 16
GLA_TAU = 16.0
GLA_CHUNK = 32
MIX_WIDTH = CONV_CH + MOBA_WIDTH + GLA_WIDTH
D_FF = 2816
FFN_CONV_WIDTH = 3
NORM_EPS = 1e-6
NEG_INF_2 = -1e30

COL_A = 2 * CONV_CH
COL_B = 3 * MOBA_WIDTH
COL_C_Q = GLA_HEADS * GLA_DK
COL_C_K = GLA_HEADS * GLA_DK
COL_C_V = GLA_WIDTH
COL_C_G = GLA_GATE_RANK
COL_C_R = GLA_WIDTH
COL_C = COL_C_Q + COL_C_K + COL_C_V + COL_C_G + COL_C_R
IN_COLS = COL_A + COL_B + COL_C


def rms_norm(x, g, eps=NORM_EPS):
    xf = x.astype(jnp.float32)
    y = xf * lax.rsqrt(jnp.mean(xf * xf, axis=-1, keepdims=True) + eps)
    return (y * g.astype(jnp.float32)).astype(x.dtype)

def head_rms_norm(x, g, n_heads):
    B, S, W = x.shape
    xf = x.astype(jnp.float32).reshape(B, S, n_heads, W // n_heads)
    y = xf * lax.rsqrt(jnp.mean(xf * xf, axis=-1, keepdims=True) + NORM_EPS)
    return (y.reshape(B, S, W) * g.astype(jnp.float32)).astype(x.dtype)

def layer_norm(x, g, b, eps=1e-5):
    xf = x.astype(jnp.float32)
    mu = jnp.mean(xf, axis=-1, keepdims=True)
    var = jnp.mean(jnp.square(xf - mu), axis=-1, keepdims=True)
    y = (xf - mu) * lax.rsqrt(var + eps)
    return (y * g.astype(jnp.float32) + b.astype(jnp.float32)).astype(x.dtype)

def causal_depthwise_conv(x, w, b):
    W = w.shape[0]
    y = lax.conv_general_dilated(
        x, w[:, None, :].astype(x.dtype), window_strides=(1,), padding=[(W - 1, 0)],
        dimension_numbers=("NWC", "WIO", "NWC"), feature_group_count=x.shape[-1])
    return y + b.astype(x.dtype)

def conformer_conv(a_val, a_gate, conv_w, conv_b, ln_g, ln_b):
    h = a_val * jax.nn.sigmoid(a_gate)
    h = causal_depthwise_conv(h, conv_w, conv_b)
    h = layer_norm(h, ln_g, ln_b)
    return jax.nn.silu(h)

def moba_attention(q, k, v):
    B, S, H, dh = q.shape
    s_pad = ((S + MOBA_BLOCK - 1) // MOBA_BLOCK) * MOBA_BLOCK
    pad = [(0, 0), (0, s_pad - S), (0, 0), (0, 0)]
    qp = jnp.pad(q, pad).transpose(0, 2, 1, 3)
    kp = jnp.pad(k, pad).transpose(0, 2, 1, 3)
    vp = jnp.pad(v, pad).transpose(0, 2, 1, 3)
    nb = s_pad // MOBA_BLOCK
    topk = min(MOBA_TOPK, nb)
    kb = kp.reshape(B, H, nb, MOBA_BLOCK, dh)
    vb = vp.reshape(B, H, nb, MOBA_BLOCK, dh)
    k_mean = jnp.mean(kb.astype(jnp.float32), axis=3)
    nq = s_pad // MOBA_Q_CHUNK
    q_chunks = qp.reshape(B, H, nq, MOBA_Q_CHUNK, dh).transpose(2, 0, 1, 3, 4)
    scale = 1.0 / math.sqrt(dh)
    chunks_per_block = MOBA_BLOCK // MOBA_Q_CHUNK
    gather_blocks = jax.vmap(jax.vmap(lambda t, i: t[i]))

    def one_chunk(args):
        c, qc = args
        own = c // chunks_per_block
        q_pos = c * MOBA_Q_CHUNK + jnp.arange(MOBA_Q_CHUNK)
        gate = jnp.einsum("bhqd,bhnd->bhqn", qc.astype(jnp.float32), k_mean)
        gate = jnp.where(jnp.arange(nb) < own, gate, NEG_INF_2)
        _, idx = lax.top_k(gate, topk)
        valid = idx < own
        ks = gather_blocks(kb, idx)
        vs = gather_blocks(vb, idx)
        l_sel = jnp.einsum("bhqd,bhqtkd->bhqtk", qc, ks).astype(jnp.float32) * scale
        l_sel = jnp.where(valid[..., None], l_sel, NEG_INF_2).reshape(B, H, MOBA_Q_CHUNK, topk * MOBA_BLOCK)
        k_own = lax.dynamic_index_in_dim(kb, own, axis=2, keepdims=False)
        v_own = lax.dynamic_index_in_dim(vb, own, axis=2, keepdims=False)
        k_pos = own * MOBA_BLOCK + jnp.arange(MOBA_BLOCK)
        l_own = jnp.einsum("bhqd,bhkd->bhqk", qc, k_own).astype(jnp.float32) * scale
        l_own = jnp.where(k_pos[None, :] <= q_pos[:, None], l_own, NEG_INF_2)
        p = jax.nn.softmax(jnp.concatenate([l_sel, l_own], axis=-1), axis=-1)
        p_sel = p[..., : topk * MOBA_BLOCK].reshape(B, H, MOBA_Q_CHUNK, topk, MOBA_BLOCK).astype(vs.dtype)
        p_own = p[..., topk * MOBA_BLOCK:].astype(v_own.dtype)
        return (jnp.einsum("bhqtk,bhqtkd->bhqd", p_sel, vs)
                + jnp.einsum("bhqk,bhkd->bhqd", p_own, v_own))

    out = lax.map(one_chunk, (jnp.arange(nq), q_chunks))
    out = out.transpose(1, 0, 3, 2, 4).reshape(B, s_pad, H, dh)
    return out[:, :S].astype(q.dtype)

def gla_chunked(q, k, v, log_a):
    B, S, H, DK = q.shape
    DV = v.shape[-1]
    C = GLA_CHUNK
    nc = S // C

    def to_chunks(t):
        return t.astype(jnp.float32).reshape(B, nc, C, H, t.shape[-1]).transpose(0, 3, 1, 2, 4)

    qc, kc, vc, gc = to_chunks(q), to_chunks(k), to_chunks(v), to_chunks(log_a)
    G = jnp.cumsum(gc, axis=3)
    gamma = G[:, :, :, -1:, :]
    qg = qc * jnp.exp(G)
    kg = kc * jnp.exp(-G)
    kd = kc * jnp.exp(gamma - G)
    tril = jnp.tril(jnp.ones((C, C), dtype=bool))
    attn = jnp.where(tril, jnp.einsum("bhnid,bhnjd->bhnij", qg, kg), 0.0)
    o_intra = jnp.einsum("bhnij,bhnje->bhnie", attn, vc)
    d_state = jnp.einsum("bhnjd,bhnje->bhnde", kd, vc)
    decay = jnp.exp(gamma[:, :, :, 0, :])

    def step(state, inp):
        d, ds = inp
        return d[..., None] * state + ds, state

    _, s_prev = lax.scan(step, jnp.zeros((B, H, DK, DV), jnp.float32),
                         (jnp.moveaxis(decay, 2, 0), jnp.moveaxis(d_state, 2, 0)))
    s_prev = jnp.moveaxis(s_prev, 0, 2)
    o = o_intra + jnp.einsum("bhnid,bhnde->bhnie", qg, s_prev)
    return o.transpose(0, 2, 3, 1, 4).reshape(B, S, H, DV).astype(v.dtype)

def second_inputs(seed: int = 0) -> dict:
    key = jax.random.key(seed)
    ks = jax.random.split(key, 20)
    f32 = jnp.float32
    n = lambda k, shape, s: jax.random.normal(k, shape, f32) * s
    return {
        "x": n(ks[0], (BATCH, SEQ, D_MODEL), 1.0),
        "norm_mix_g": 1.0 + n(ks[1], (DEPTH, D_MODEL), 0.05),
        "w_in": n(ks[2], (DEPTH, D_MODEL, IN_COLS), D_MODEL ** -0.5),
        "conv_w": n(ks[3], (DEPTH, CONV_WIDTH, CONV_CH), CONV_WIDTH ** -0.5),
        "conv_b": n(ks[4], (DEPTH, CONV_CH), 0.02),
        "conv_ln_g": 1.0 + n(ks[5], (DEPTH, CONV_CH), 0.05),
        "conv_ln_b": n(ks[6], (DEPTH, CONV_CH), 0.02),
        "moba_out_g": 1.0 + n(ks[7], (DEPTH, MOBA_WIDTH), 0.05),
        "gla_gate_w": n(ks[8], (DEPTH, GLA_GATE_RANK, GLA_HEADS * GLA_DK), GLA_GATE_RANK ** -0.5),
        "gla_gate_b": n(ks[9], (DEPTH, GLA_HEADS * GLA_DK), 0.1),
        "gla_out_g": 1.0 + n(ks[10], (DEPTH, GLA_WIDTH), 0.05),
        "w_out": n(ks[11], (DEPTH, MIX_WIDTH, D_MODEL), MIX_WIDTH ** -0.5),
        "norm_ffn_g": 1.0 + n(ks[12], (DEPTH, D_MODEL), 0.05),
        "ffn_w_up": n(ks[13], (DEPTH, D_MODEL, 2 * D_FF), D_MODEL ** -0.5),
        "ffn_conv_w": n(ks[14], (DEPTH, FFN_CONV_WIDTH, 2 * D_FF), FFN_CONV_WIDTH ** -0.5),
        "ffn_conv_b": n(ks[15], (DEPTH, 2 * D_FF), 0.02),
        "ffn_w_down": n(ks[16], (DEPTH, D_FF, D_MODEL), D_FF ** -0.5),
        "final_g": 1.0 + n(ks[17], (D_MODEL,), 0.05),
    }

def second_block(x, norm_mix_g, w_in, conv_w, conv_b, conv_ln_g, conv_ln_b, moba_out_g,
              gla_gate_w, gla_gate_b, gla_out_g, w_out, norm_ffn_g, ffn_w_up, ffn_conv_w,
              ffn_conv_b, ffn_w_down, final_g):
    B, S, _ = x.shape
    o1 = COL_A
    o2 = o1 + COL_B
    o3 = o2 + COL_C_Q
    o4 = o3 + COL_C_K
    o5 = o4 + COL_C_V
    o6 = o5 + COL_C_G
    for l in range(DEPTH):
        h = rms_norm(x, norm_mix_g[l])
        p = h @ w_in[l].astype(h.dtype)
        y_a = conformer_conv(p[..., :CONV_CH], p[..., CONV_CH:o1],
                             conv_w[l], conv_b[l], conv_ln_g[l], conv_ln_b[l])
        qkv = p[..., o1:o2].reshape(B, S, 3, MOBA_HEADS, MOBA_HEAD_DIM)
        y_b = moba_attention(qkv[:, :, 0], qkv[:, :, 1], qkv[:, :, 2]).reshape(B, S, MOBA_WIDTH)
        y_b = head_rms_norm(y_b, moba_out_g[l], MOBA_HEADS)
        q_c = p[..., o2:o3].reshape(B, S, GLA_HEADS, GLA_DK) * (GLA_DK ** -0.5)
        k_c = p[..., o3:o4].reshape(B, S, GLA_HEADS, GLA_DK)
        v_c = p[..., o4:o5].reshape(B, S, GLA_HEADS, GLA_DV)
        gate_logit = (p[..., o5:o6] @ gla_gate_w[l].astype(p.dtype)).astype(jnp.float32) \
            + gla_gate_b[l].astype(jnp.float32)
        log_a = (jax.nn.log_sigmoid(gate_logit) / GLA_TAU).reshape(B, S, GLA_HEADS, GLA_DK)
        y_c = gla_chunked(q_c, k_c, v_c, log_a).reshape(B, S, GLA_WIDTH)
        y_c = head_rms_norm(y_c, gla_out_g[l], GLA_HEADS) * jax.nn.silu(p[..., o6:])
        y = jnp.concatenate([y_a, y_b, y_c], axis=-1) @ w_out[l].astype(x.dtype)
        x = x + y
        h = rms_norm(x, norm_ffn_g[l])
        u = causal_depthwise_conv(h @ ffn_w_up[l].astype(h.dtype), ffn_conv_w[l], ffn_conv_b[l])
        x = x + (jax.nn.silu(u[..., :D_FF]) * u[..., D_FF:]) @ ffn_w_down[l].astype(x.dtype)
    return rms_norm(x, final_g)


def setup_inputs(seed=0):
    out = dict(first_inputs(seed))
    for name, value in second_inputs(seed + 1).items():
        if name != "x":
            out[name + "_2"] = value
    return out


def reference(
    x, a_norm, a_w_in, a_sgu_norm, a_w_spatial, a_b_spatial, a_w_out, kv_norm, w_kv, b_norm,
    b_w_q, b_rel_bias, b_w_o, ffn_norm, ffn_w_gate_up, ffn_w_down, final_norm, norm_mix_g_2,
    w_in_2, conv_w_2, conv_b_2, conv_ln_g_2, conv_ln_b_2, moba_out_g_2, gla_gate_w_2,
    gla_gate_b_2, gla_out_g_2, w_out_2, norm_ffn_g_2, ffn_w_up_2, ffn_conv_w_2, ffn_conv_b_2,
    ffn_w_down_2, final_g_2,
):
    x = first_block(
        x, a_norm, a_w_in, a_sgu_norm, a_w_spatial, a_b_spatial, a_w_out, kv_norm, w_kv, b_norm,
        b_w_q, b_rel_bias, b_w_o, ffn_norm, ffn_w_gate_up, ffn_w_down, final_norm,
    )
    return second_block(
        x, norm_mix_g_2, w_in_2, conv_w_2, conv_b_2, conv_ln_g_2, conv_ln_b_2, moba_out_g_2,
        gla_gate_w_2, gla_gate_b_2, gla_out_g_2, w_out_2, norm_ffn_g_2, ffn_w_up_2,
        ffn_conv_w_2, ffn_conv_b_2, ffn_w_down_2, final_g_2,
    )


_drawn_inputs = setup_inputs


def setup_inputs(seed=0):
    import zlib

    import numpy as np

    out = dict(_drawn_inputs(seed))
    spreads = {}
    factors = {'a_sgu_norm': 4.077,
     'kv_norm': 6.094,
     'b_norm': 8.0,
     'b_rel_bias': 3.802,
     'conv_b_2': 2.864,
     'conv_ln_b_2': 6.536,
     'ffn_conv_b_2': 3.083}
    for name, (base, spread) in spreads.items():
        noise = np.random.default_rng([zlib.crc32(name.encode()), seed]).standard_normal(out[name].shape)
        drawn = base * np.exp(spread * noise) if base else spread * noise
        out[name] = __import__('jax').numpy.asarray(drawn.astype(out[name].dtype))
    for name, factor in factors.items():
        out[name] = (out[name] * factor).astype(out[name].dtype)
    return out
```

```python
from contextlib import ExitStack

import numpy as np

import concourse.bass as bass
from concourse import mybir

P = 128
F32 = mybir.dt.float32
F32R = mybir.dt.float32r
U32 = mybir.dt.uint32
ALU = mybir.AluOpType
ACT = mybir.ActivationFunctionType
AX = mybir.AxisListType

D = 1024
SEQ = 256
M = SEQ // P
KT = D // P
DFF_A = 2 * D
GROUPS = 8
GDIM = DFF_A // GROUPS
HID = 2816
CTF = HID // 256
HEADS, DH = 16, 64
CHUNK = 64
NEG = -1e30
MAX_REL = 256
CONV_CH, TAPS = 256, 31
GH, DK, DV = 4, 64, 128
GCH = 32
NCH = SEQ // GCH
RANK = 16
TAU = 16.0
EPS, LN_EPS = 1e-6, 1e-5
SLOTS = 4
UNIT = 2048

U_IN = 0
U_OUTA = U_IN + 16
U_GLU0 = U_OUTA + 8
U_DOWN0 = U_GLU0 + 2 * CTF
U_KVQ = U_DOWN0 + CTF
U_WO = U_KVQ + 12
U_GLU1 = U_WO + 4
U_DOWN1 = U_GLU1 + 2 * CTF
U_MIX = U_DOWN1 + CTF
MIX_ORDER = (0, 2, 3, 1)
MIX_END = (2, 4, 6, 8, 9, 11)
POOL_TAPS = 20
PER_LAYER = 11 + 4 + 2 * CTF + CTF
TOTAL = U_MIX + 2 * PER_LAYER

C_IN, C_GLU0, C_KVQ = 0, 8, 8 + CTF
C_GLU1 = C_KVQ + 6
C_MIX = C_GLU1 + CTF
C_LAYER = 6 + CTF



def two_blocks_kernel(nc, x_in, stream, cols, bs_col, ws_t, gs_row, fin_row, fin2_row, rel_rows, ffn_cw,
                      conv_w, conv_ln, moba_g, gla_g, gate_w, gate_b, gate_in, out):
    ctx = ExitStack()
    with ctx:
        def sem(name):
            return ctx.enter_context(nc.semaphore(name))

        base = 16512

        def at(name, shape, offset, dt=F32):
            return nc.alloc_sbuf_tensor_at(name, [P] + shape, dt, offset=base + 4 * offset)

        o_raw, o_hi, o_lo = 0, SLOTS * UNIT, 2 * SLOTS * UNIT
        o_x = 3 * SLOTS * UNIT
        o_xh = o_x + M * D
        o_xl = o_xh + KT * SEQ
        o_yh = o_xl + KT * SEQ
        o_yl = o_yh + 22 * SEQ
        o_sc = o_yl + 22 * SEQ
        o_c = o_sc + 9216
        o_sa, o_sb = o_yh + KT * SEQ, o_yl + KT * SEQ

        raw = at("raw", [SLOTS, UNIT], o_raw)
        whi = at("whi", [SLOTS, UNIT], o_hi, F32R)
        wlo = at("wlo", [SLOTS, UNIT], o_lo, F32R)
        x = at("x", [M, D], o_x)
        xth = at("xth", [KT, SEQ], o_xh, F32R)
        xtl = at("xtl", [KT, SEQ], o_xl, F32R)
        yth = at("yth", [22 * SEQ], o_yh, F32R)
        ytl = at("ytl", [22 * SEQ], o_yl, F32R)
        yth3 = yth[:, :].rearrange("p (k t) -> p k t", t=SEQ)
        ytl3 = ytl[:, :].rearrange("p (k t) -> p k t", t=SEQ)

        c_at = [o_c]

        def const(name, shape, dt=F32):
            n = -(-int(np.prod(shape)) // 8) * 8
            c_at[0] += n
            assert base + 4 * c_at[0] <= 229344
            return at(name, shape, c_at[0] - n, dt)

        ident = const("ident", [P])
        cmask = const("cmask", [2 * P])
        tri = const("tri", [P])
        ones = const("ones", [P])
        mhalf = const("mhalf", [8])
        gcol = const("gcol", [9, KT])
        bsc = const("bsc", [GROUPS])
        fcw = const("fcw", [2, CTF * 16])
        cw = const("cw", [2, 2, 32])
        cln = const("cln", [2, 2, 2])
        mog = const("mog", [2, 2])
        glg = const("glg", [2, 4])
        stat = const("stat", [320])
        bnst = const("bnst", [2, 8])
        mvv = const("mvv", [2, 2])
        dec = const("dec", [2, NCH])

        xg = at("xg", [4, 512], o_sc + 6144)
        junk = at("junk", [1024], o_sc + 8192)
        frow = at("frow", [D], o_sc + 4096)
        v_a = at("v_a", [M, DFF_A], o_sc)
        ws_sb = at("ws_sb", [GROUPS, P], o_sc + 4096)
        gs_sb = at("gs_sb", [DFF_A], o_sc + 5120)
        ug = at("ug", [2, M, 512], o_sc + 7168)
        xg0 = at("xg0", [4, 512], o_sa)
        junk0 = at("junk0", [1024], o_sb)
        sg = at("sg", [2, M, 256], o_sc)
        yy = at("yy", [2, M, 256], o_sc + 1024)
        us = at("us", [2, M, 512], o_sc)
        cv = at("cv", [2, 4, SEQ], o_sc + 2048)
        pr = at("pr", [2, 2, SEQ], o_sc + 4096)
        kT = at("kT", [KT, SEQ], o_sc)
        qT = at("qT", [KT, SEQ], o_sc + 2048)
        vt = at("vt", [M, D], o_sc + 4096)
        st = at("st", [M, 512], o_yh + 16 * SEQ)
        sb1 = at("sb1", [2, 384], o_sc + 6144)
        pt1 = at("pt1", [2, 384], o_sc + 6912)
        rb = at("rb", [2, 2, SEQ], o_sc + 7680)
        hpad = at("hpad", [2, TAPS - 1 + SEQ], o_sc)
        cacc = at("cacc", [2, SEQ], o_sc + 576)
        sgc = at("sgc", [M, 256], o_sc + 1088)
        hc = at("hc", [M, 256], o_sc + 1600)
        mqk = at("mqk", [M, 512], o_sc + 1088)
        pt2 = at("pt2", [2, 384], o_sc + 1088)
        gqk = at("gqk", [M, 512], o_sc + 2112)
        sb2 = at("sb2", [2, 384], o_sc + 2112)
        gv = at("gv", [M, 512], o_sc + 3136)
        rs = at("rs", [M, 512], o_sc + 4160)
        gG = at("gG", [2, SEQ], o_sc + 5184)
        eG = at("eG", [2, SEQ], o_sc + 5696)
        nG = at("nG", [2, SEQ], o_sc + 6208)
        dG = at("dG", [2, SEQ], o_sc + 6720)
        kdt = at("kdt", [M, 256], o_sc + 5184)
        aT = at("aT", [M, 512], o_sc + 7232)
        la = at("la", [M, 256], o_sc + 8256)
        ycs = at("ycs", [2, SEQ], o_sc + 8256)
        st_g = at("st_g", [NCH - 1, 2, P], o_sa)
        osq = at("osq", [M, 512], o_sa)
        mqT = at("mqT", [2, SEQ], o_sa + 1792)
        mkT = at("mkT", [2, SEQ], o_sa + 2304)
        mv = at("mv", [M, 256], o_sa + 2816)
        g16 = at("g16", [M, RANK], o_sa + 3328)
        gw_sb = at("gw_sb", [256], o_sb)
        gb_sb = at("gb_sb", [256], o_sb + 256)
        gin = at("gin", [KT * RANK], o_sb + 512)
        ginh = at("ginh", [KT * RANK], o_sb + 640, F32R)
        ginl = at("ginl", [KT * RANK], o_sb + 768, F32R)
        gT = at("gT", [SEQ], o_sb + 896)
        tmp = at("tmp", [M, 256], o_sb + 1152)
        cvn = at("cvn", [M, 256], o_sb + 1152)
        og = at("og", [M, 512], o_sb + 1664)
        mo = at("mo", [M, 256], o_sb + 2688)
        msq = at("msq", [M, 256], o_sc + 6720)
        ptap = at("ptap", [SEQ], o_sc + 8768)
        cacc2 = at("cacc2", [SEQ], o_sb + 3200)

        acc = [ctx.enter_context(nc.psum_tensor(f"acc{i}", [P, 512], F32)) for i in range(4)]
        tb = [ctx.enter_context(nc.psum_tensor(f"tb{i}", [P, 512], F32)) for i in range(4)]

        raw_ready = [sem(f"raw_ready{i}") for i in range(SLOTS)]
        hi_ready, lo_ready, unit_used = sem("hi_ready"), sem("lo_ready"), sem("unit_used")
        m0_done, out_group = sem("m0_done"), sem("out_group")
        x_loaded = [sem(f"x_loaded{m}") for m in range(M)]
        gains_loaded, consts_loaded, consts_made, made = (
            sem(n) for n in ("gains_loaded", "consts_loaded", "consts_made", "made"))
        n_add, n_tr, n_gm, n_hi, n_lo, n_sq, n_ms, n_r = (
            sem("norm_" + n) for n in ("added", "transposed", "gained", "hi", "lo", "squared", "meaned", "rms"))
        q_gm, q_hi, q_lo = sem("qnorm_gained"), sem("qnorm_hi"), sem("qnorm_lo")
        f_row, f_app, f_out = sem("final_row"), sem("final_applied"), sem("out_stored")
        f_ms, f_rt = sem("final_meaned"), sem("final_rms")
        a_ev, a_vsq, a_vsum, a_ms, a_r, a_vn, a_sp, a_spc, a_y, a_tr, a_hi, a_lo = (
            sem("gmlp_" + n) for n in ("act", "v_squared", "v_summed", "v_meaned", "v_rms", "v_normed", "spatial",
                                       "spatial_kept", "gated", "transposed", "hi", "lo"))
        g_silu, g_mul, g_tr, g_hi, g_lo = (sem("glu_" + n) for n in ("silu", "gated", "transposed", "hi", "lo"))
        k_ev, k_tr, k_cp = (sem("kvq_" + n) for n in ("kept", "transposed", "copied"))
        rb_ld, rb_ok = sem("relbias_loaded"), sem("relbias_masked")
        t_s, t_sb, t_mx, t_p, t_rd, t_pt, t_ptc, t_o, t_on = (
            sem("attn_" + n) for n in ("scores", "biased", "max", "exp", "denominator", "p_transposed", "p_kept",
                                       "pv", "normed"))
        w_tr, w_hi, w_lo = (sem("attn_out_" + n) for n in ("transposed", "hi", "lo"))
        f_ev, f_tr, f_t0, f_t1, f_t2, f_si, f_pr, f_hi, f_lo = (
            sem("ffn_" + n) for n in ("kept", "transposed", "tap2", "tap1", "tap0", "silu", "product", "hi", "lo"))
        x_ld, x_gh, x_gl = sem("gate_loaded"), sem("gate_hi"), sem("gate_lo")
        x_pad, x_sig, x_gated, x_ctr, x_cpad, x_tap = (
            sem("conv_" + n) for n in ("padded", "sigmoid", "gated", "transposed", "kept", "tap"))
        x_ltr, x_bn, x_ag, x_lms, x_lr, x_nrm, x_btr, x_sl = (
            sem("conv_ln_" + n) for n in ("transposed", "stats", "mean", "var", "rstd", "normed", "back", "silu"))
        x_ev = sem("mix_kept")
        x_g16, x_g16c, x_gT, x_gTc, x_lg, x_ab, x_ex, x_ln, x_la, x_cs = (
            sem("gla_" + n) for n in ("gate_in", "gate_kept", "gate_transposed", "gate_t_kept", "logit", "abs", "exp",
                                      "log", "log_a", "cumsum"))
        x_qktr, x_G, x_e1, x_gd, x_e2, x_qg, x_kd, x_kdtr, x_kdc = (
            sem("gla_" + n) for n in ("qk_transposed", "G_kept", "exp_G", "G_diff", "exp_diff", "q_decayed", "k_decayed",
                                      "kd_transposed", "kd_kept"))
        x_at0, x_A, x_Am, x_dS, x_St, x_o, x_oc = (
            sem("gla_" + n) for n in ("masked_zeroed", "scores", "scores_masked", "state_inc", "state", "o", "o_kept"))
        x_osq, x_oss, x_oms, x_or, x_on, x_ytr, x_yg, x_yh, x_yl = (
            sem("head_" + n) for n in ("squared", "summed", "meaned", "rms", "normed", "y_transposed", "y_gained",
                                       "y_hi", "y_lo"))
        x_on2 = sem("head_gated")
        x_mtr, x_mcp = sem("moba_transposed"), sem("moba_kept")
        x_pm, x_pa, x_tap1 = sem("conv_pool_product"), sem("conv_pool_sum"), sem("conv_tap_second")

        block = ctx.enter_context(nc.Block())

        def gu(l):
            return U_MIX + PER_LAYER * l

        def gc(l):
            return C_MIX + C_LAYER * l

        def rms(k, m):
            return stat[:, 2 * k + m:2 * k + m + 1]

        def ssq(k, m, n=1):
            return stat[:, 40 + 2 * k + m:40 + 2 * k + m + n]

        STATS = {0: 0, 1: 1, 2: 2, 3: 3, 4: 5, 5: 6, 6: 7, 7: 8}
        FIN1, FIN2 = 4, 9
        ROUNDS = 10

        def pair_bank(pair, m):
            return acc[(pair % 2) * 2 + m]

        PAIR_IN, PAIR_OUTA = 0, 0
        PAIR_GLU0 = 0
        PAIR_DOWN0 = (PAIR_GLU0 + CTF) % 2
        PAIR_KVQ = PAIR_DOWN0
        PAIR_WO = PAIR_KVQ
        PAIR_GLU1 = PAIR_WO
        PAIR_DOWN1 = (PAIR_GLU1 + CTF) % 2

        def pair_mix(l):
            return (PAIR_DOWN1 + l) % 2

        def pair_fdown(l):
            return (pair_mix(l) + CTF) % 2

        KQ_BANK = [(tb[0], tb[1]), (tb[2], tb[3]), (tb[3], tb[3]), (tb[0], tb[1])]

        def out_bank(pair, m, c):
            return acc[((m + pair) % 2) * 2 + c]

        def wait_group(eng, ct, u, m, t=0):
            if m == 0:
                eng.wait_ge(m0_done, ct + 1 + 2 * t)
            else:
                eng.wait_ge(unit_used, u + 4 * t)

        def wait_out(eng, k, u_end, q):
            if q < 3:
                eng.wait_ge(out_group, 3 * (k - 1) + q + 1)
            else:
                eng.wait_ge(unit_used, u_end)

        OUT_END = {1: U_GLU0, 2: U_KVQ, 3: U_GLU1, 4: U_MIX, 5: gu(0) + 15, 6: gu(1), 7: gu(1) + 15, 8: TOTAL}
        OUT_PAIR = {1: PAIR_OUTA, 2: PAIR_DOWN0, 3: PAIR_WO, 4: PAIR_DOWN1, 5: pair_mix(0), 6: pair_fdown(0),
                    7: pair_mix(1), 8: pair_fdown(1)}

        @block.sync
        def _(sp):
            for u in range(SLOTS):
                if u < M:
                    sp.dma_start(x[:, u, :], x_in[u * P:(u + 1) * P, :]).then_inc(x_loaded[u], 16)
                sp.dma_start(raw[:, u, :], stream[u]).then_inc(raw_ready[u], 16)
            groups = TOTAL // SLOTS - 1
            with sp.Fori(0, groups) as t:
                for j in range(SLOTS):
                    sp.wait_ge(lo_ready, SLOTS * t + j + 1)
                    sp.dma_start(raw[:, j, :], stream[SLOTS * t + (SLOTS + j)]).then_inc(raw_ready[j], 16)
            for u in range(SLOTS * (groups + 1), TOTAL):
                sp.wait_ge(lo_ready, u - SLOTS + 1)
                sp.dma_start(raw[:, u % SLOTS, :], stream[u]).then_inc(raw_ready[u % SLOTS], 16)
            for m in range(M):
                sp.wait_ge(f_app, M + m + 1)
                sp.dma_start(out[m * P:(m + 1) * P, :], x[:, m, :]).then_inc(f_out, 16)
            sp.wait_ge(f_out, 16 * M)

        @block.gpsimd
        def _(pool):
            pool.memset(ident[:, :], 1.0).then_inc(made, 1)
            pool.memset(cmask[:, :], 0.0).then_inc(made, 1)
            pool.memset(tri[:, :], 1.0).then_inc(made, 1)
            pool.memset(ones[:, :], 1.0).then_inc(made, 1)
            pool.memset(mhalf[:, :], -0.5).then_inc(made, 1)
            pool.wait_ge(made, 5)
            pool.affine_select(out=ident[:, :], in_=ident[:, :], compare_op=ALU.is_equal, fill=0.0, base=0,
                               pattern=[[-1, P]], channel_multiplier=1).then_inc(consts_made, 1)
            pool.affine_select(out=cmask[:, P:2 * P], in_=cmask[:, P:2 * P], compare_op=ALU.is_ge, fill=NEG, base=0,
                               pattern=[[-1, P]], channel_multiplier=1).then_inc(consts_made, 1)
            pool.affine_select(out=tri[:, :], in_=tri[:, :], compare_op=ALU.is_ge, fill=0.0, base=0,
                               pattern=[[1, P]], channel_multiplier=-1).then_inc(made, 1)
            pool.wait_ge(made, 6)
            t3 = tri[:, :].rearrange("p (b c) -> p b c", c=GCH)
            pool.affine_select(out=t3, in_=t3, compare_op=ALU.is_ge, fill=0.0, base=0,
                               pattern=[[-GCH, P // GCH], [0, GCH]], channel_multiplier=1).then_inc(consts_made, 1)

            def root(r):
                pool.wait_ge(n_sq, 2 * r + 2)
                pool.tensor_scalar(ssq(r, 0, 2), ssq(r, 0, 2), 1.0 / D, EPS, ALU.mult, ALU.add).then_inc(n_ms, 1)
                pool.wait_ge(n_ms, r + 1)
                pool.tensor_tensor(stat[:, 2 * r:2 * r + 2], ssq(r, 0, 2), mhalf[:, 0:2], ALU.pow).then_inc(n_r, 1)

            pool.wait_ge(consts_made, 3)
            def final_root(r, e):
                for m, (mean, done, n) in enumerate(((f_ms, f_rt, e), (n_ms, n_r, r))):
                    pool.wait_ge(n_sq, 2 * r + m + 1)
                    pool.tensor_scalar(ssq(r, m), ssq(r, m), 1.0 / D, EPS, ALU.mult, ALU.add).then_inc(mean, 1)
                    pool.wait_ge(mean, n + 1)
                    pool.tensor_tensor(rms(r, m), ssq(r, m), mhalf[:, 0:1], ALU.pow).then_inc(done, 1)

            root(0)
            pool.dma_start(ws_sb[:, :, :], ws_t).then_inc(consts_loaded, 16)
            pool.dma_start(gs_sb[:, :], gs_row.to_broadcast([P, DFF_A])).then_inc(consts_loaded, 16)
            pool.dma_start(bsc[:, :], bs_col).then_inc(consts_loaded, 16)
            pool.dma_start(fcw[:, :, :], ffn_cw).then_inc(consts_loaded, 16)
            pool.dma_start(cw[:, :, :, :], conv_w).then_inc(consts_loaded, 16)
            pool.dma_start(cln[:, :, :, :], conv_ln).then_inc(consts_loaded, 16)
            pool.dma_start(mog[:, :, :], moba_g).then_inc(consts_loaded, 16)
            pool.dma_start(glg[:, :, :], gla_g).then_inc(consts_loaded, 16)
            pool.wait_ge(consts_loaded, 16 * 8)
            pool.wait_ge(n_r, 1)
            pool.memset(ws_sb[CHUNK:P, :, 0:CHUNK], 0.0).then_inc(consts_made, 1)
            pool.wait_ge(consts_made, 4)
            pool.wait_ge(a_vsum, 1)
            pool.tensor_scalar(stat[:, 66:68], stat[:, 64:66], 1.0 / DFF_A, EPS, ALU.mult, ALU.add).then_inc(a_ms, 1)
            pool.wait_ge(a_ms, 1)
            pool.tensor_tensor(stat[:, 68:70], stat[:, 66:68], mhalf[:, 0:2], ALU.pow).then_inc(a_r, 1)
            root(1)
            root(2)
            for c in range(HEADS // 2):
                if c == 0:
                    pool.wait_ge(q_lo, 4)
                    pool.wait_ge(n_sq, 2 * 2 + 2)
                if c >= 2:
                    pool.wait_ge(t_sb, 2 * (c - 2) + 2)
                pool.dma_start(rb[:, c % 2, :, :], rel_rows[:, 2 * c:2 * c + 2, :]).then_inc(rb_ld, 16)
                pool.wait_ge(rb_ld, 16 * (c + 1))
                pool.memset(rb[0:CHUNK, c % 2, :, P + CHUNK:2 * P], NEG).then_inc(rb_ok, 1)
            root(3)
            pool.wait_ge(g_lo, 2 * CTF)
            pool.dma_start(frow[:, :], fin_row.to_broadcast([P, D])).then_inc(f_row, 16)
            final_root(FIN1, 0)
            def head_root(l, i, w):
                pool.wait_ge(x_oss, 2 * l + i + 1)
                pool.tensor_scalar(stat[:, 80 + 8 * i:88 + 8 * i], stat[:, 96 + 8 * i:104 + 8 * i], 1.0 / w, EPS,
                                   ALU.mult, ALU.add).then_inc(x_oms, 1)
                pool.wait_ge(x_oms, 2 * l + i + 1)
                pool.tensor_tensor(stat[:, 112 + 8 * i:120 + 8 * i], stat[:, 80 + 8 * i:88 + 8 * i], mhalf[:, 0:8],
                                   ALU.pow).then_inc(x_or, 1)

            for l in range(2):
                pool.wait_ge(unit_used, gu(l))
                pool.dma_start(gw_sb[0:RANK, :], gate_w[l]).then_inc(x_ld, 16)
                pool.dma_start(gb_sb[0:1, :], gate_b[l]).then_inc(x_ld, 16)
                pool.dma_start(gin[:, :], gate_in[l]).then_inc(x_ld, 16)
                root(STATS[4 + 2 * l])
                pool.memset(hpad[:, :, 0:TAPS - 1], 0.0).then_inc(x_pad, 1)
                pool.wait_ge(n_lo, 4 * (4 + 2 * l) + 4)
                pool.wait_ge(n_sq, 2 * STATS[4 + 2 * l] + 2)
                pool.memset(aT[:, :, :], 0.0).then_inc(x_at0, 1)
                pool.wait_ge(x_cpad, l + 1)
                for i in range(POOL_TAPS):
                    dst = ptap if i else cacc2
                    if i > 1:
                        pool.wait_ge(x_pa, (POOL_TAPS - 1) * l + i - 1)
                    pool.tensor_scalar(dst[:, :], hpad[:, 1, i:i + SEQ], cw[:, l, 1, i:i + 1], None,
                                       ALU.mult).then_inc(x_pm, 1)
                    pool.wait_ge(x_pm, POOL_TAPS * l + i + 1)
                    if i:
                        pool.tensor_tensor(cacc2[:, :], cacc2[:, :], ptap[:, :], ALU.add).then_inc(x_pa, 1)
                pool.wait_ge(x_ag, 2 * l + 2)
                pool.tensor_scalar(stat[:, 72:74], mvv[:, :, 1], 1.0, LN_EPS, ALU.mult, ALU.add).then_inc(x_lms, 1)
                pool.wait_ge(x_lms, l + 1)
                pool.tensor_tensor(stat[:, 74:76], stat[:, 72:74], mhalf[:, 0:2], ALU.pow).then_inc(x_lr, 1)
                head_root(l, 0, DV)
                head_root(l, 1, DH)
                root(6 + 2 * l)
                if l == 1:
                    pool.wait_ge(f_lo, 2 * CTF)
                    pool.dma_start(frow[:, :], fin2_row.to_broadcast([P, D])).then_inc(f_row, 16)
                if l == 1:
                    final_root(FIN2, 1)

        @block.scalar
        def _(act):
            act.dma_start(gcol[:, :, :], cols).then_inc(gains_loaded, 16)

            def hi(U, t=0):
                if U >= TOTAL:
                    return
                s = U % SLOTS
                act.wait_ge(raw_ready[s], 16 * (U // SLOTS + 1) + 16 * t)
                if U >= SLOTS:
                    act.wait_ge(unit_used, U - SLOTS + 1 + 4 * t)
                act.activation(whi[:, s, :], raw[:, s, :], ACT.Copy).then_inc(hi_ready, 1)

            def norm_hi(k, q):
                m, c = divmod(q, 2)
                act.wait_ge(n_gm, 4 * k + q + 1)
                act.activation(xth[:, 4 * c:4 * c + 4, m * P:(m + 1) * P],
                               (xg0 if k == 0 else xg)[:, q, :].rearrange("p (k t) -> p k t", t=P),
                               ACT.Copy).then_inc(n_hi, 1)

            def square(r, m, after=None, n=0, jk=None):
                if after is not None:
                    act.wait_ge(after, n)
                if m == 1 or r > 0:
                    act.wait_ge(n_sq, 2 * r + m)
                act.activation((jk if jk is not None else junk)[:, :], x[:, m, :], ACT.Square, accum_out=ssq(r, m)).then_inc(n_sq, 1)

            def norm(k):
                for q in range(4):
                    norm_hi(k, q)
                if k != 4:
                    for m in range(M):
                        square(STATS[k], m, n_add, 4 * (k - 1) + 2 * m + 2)

            norm_hi(0, 0)
            norm_hi(0, 1)
            hi(0)
            hi(1)
            norm_hi(0, 2)
            norm_hi(0, 3)
            for m in range(M):
                square(0, m, x_loaded[m], 16, jk=junk0)

            def gmlp_act(j):
                for m in range(M):
                    wait_group(act, C_IN + j, U_IN + 2 * j + 2, m)
                    if j == 0 and m == 0:
                        act.wait_ge(n_r, 1)
                    if j < 4:
                        o = v_a[:, m, 512 * j:512 * j + 512]
                    else:
                        if j >= 6:
                            act.wait_ge(a_tr, 2 * (j - 6) + 2)
                        o = ug[:, j % 2, m, :]
                    act.activation(o, pair_bank(j + PAIR_IN, m)[:, :], ACT.Gelu, scale=rms(0, m)).then_inc(a_ev, 1)
                if j < 4:
                    for m in range(M):
                        act.wait_ge(a_ev, 2 * j + m + 1)
                        if j or m:
                            act.wait_ge(a_vsq, 2 * j + m)
                        act.activation(junk0[:, 0:512], v_a[:, m, 512 * j:512 * j + 512], ACT.Square,
                                       accum_out=stat[:, 128 + 4 * m + j:129 + 4 * m + j]).then_inc(a_vsq, 1)

            def spatial_keep(m):
                for b in range(4):
                    act.wait_ge(a_sp, 4 * m + b + 1)
                    act.activation(v_a[:, m, 512 * b:512 * b + 512], tb[b][:, :], ACT.Copy).then_inc(a_spc, 1)

            def gmlp_hi(jj):
                for m in range(M):
                    act.wait_ge(a_tr, 2 * jj + m + 1)
                    act.activation(yth3[:, 4 * jj:4 * jj + 4, m * P:(m + 1) * P],
                                   tb[2 * (jj % 2) + m][:, :].rearrange("p (k t) -> p k t", t=P),
                                   ACT.Copy).then_inc(a_hi, 1)

            hi(2)
            hi(3)
            for j in range(1, 8):
                gmlp_act(j - 1)
                hi(2 * j + 2)
                if j == 5:
                    spatial_keep(0)
                hi(2 * j + 3)
                if j == 5:
                    spatial_keep(1)
                if j == 6:
                    gmlp_hi(0)
                if j == 7:
                    gmlp_hi(1)
                    gmlp_hi(2)
            for j in range(8):
                if j == 0:
                    gmlp_act(7)
                hi(U_OUTA + j + 2)
                if j == 0:
                    gmlp_hi(3)
            norm(1)

            def glu(e, U0, C0, k, pair):
                def silu(j, t=0):
                    for m in range(M):
                        wait_group(act, C0 + j, U0 + 2 * j + 2, m, t)
                        if j == 0 and m == 0:
                            act.wait_ge(n_r, STATS[k] + 1)
                        act.activation(sg[:, j % 2, m, :], pair_bank(j + pair, m)[:, 0:256], ACT.Silu,
                                       scale=rms(STATS[k], m)).then_inc(g_silu, 1)

                def keep(j, t=0):
                    act.wait_ge(g_tr, CTF * e + j + 1 + 2 * t)
                    act.activation(yth[:, bass.ds((2 * j + 4 * t) * SEQ, 512)], tb[j % 2][:, :], ACT.Copy).then_inc(g_hi, 1)

                hi(U0 + 2)
                hi(U0 + 3)
                for j in (1, 2):
                    silu(j - 1)
                    hi(U0 + 2 * j + 2)
                    hi(U0 + 2 * j + 3)
                    keep(j - 1)
                with act.Fori(0, (CTF - 3) // 2) as t:
                    for j in (3, 4):
                        silu(j - 1, t)
                        hi(U0 + 2 * j + 2, t)
                        hi(U0 + 2 * j + 3, t)
                        keep(j - 1, t)
                silu(CTF - 1)
                hi(U0 + 2 * CTF + 2)
                keep(CTF - 1)
                for j in range(1, CTF):
                    hi(U0 + 2 * CTF + j + 2)

            glu(0, U_GLU0, C_GLU0, 1, PAIR_GLU0)
            norm(2)
            hi(U_KVQ + 2)
            hi(U_KVQ + 3)
            for q in range(4):
                m, c = divmod(q, 2)
                act.wait_ge(q_gm, q + 1)
                act.activation(yth3[:, 4 * c:4 * c + 4, m * P:(m + 1) * P],
                               xg[:, q, :].rearrange("p (k t) -> p k t", t=P), ACT.Copy).then_inc(q_hi, 1)

            def kvq_keep(j):
                for m in range(M):
                    wait_group(act, C_KVQ + j, U_KVQ + 2 * j + 2, m)
                    if j == 0 and m == 0:
                        act.wait_ge(n_r, STATS[2] + 1)
                        act.wait_ge(q_lo, 4)
                    if j % 3 == 1:
                        o = vt[:, m, 512 * (j // 3):512 * (j // 3) + 512]
                    else:
                        i = (0, 0, 1, 2, 0, 3)[j]
                        if i:
                            act.wait_ge(k_tr, 2 * (i - 1) + m + 1)
                        o = st[:, m, :]
                    act.activation(o, pair_bank(j + PAIR_KVQ, m)[:, :], ACT.Copy, scale=rms(STATS[2], m)).then_inc(k_ev, 1)

            def heads(h0, n, sb, pt, s0, banks):
                def keep(i):
                    h = h0 + i
                    act.wait_ge(t_pt, h + 1)
                    if i >= 2:
                        act.wait_ge(t_o, h - 1)
                    act.activation(pt[:, i % 2, :], banks[i % 2][:, 0:384], ACT.Copy).then_inc(t_ptc, 1)

                def exp(i):
                    h = h0 + i
                    for m in range(M):
                        act.wait_ge(t_mx, 2 * h + m + 1)
                        w = sb[:, i % 2, 0:P] if m == 0 else sb[:, i % 2, P:3 * P]
                        act.activation(w, w, ACT.Exp, bias=stat[:, s0 + 2 * i + m:s0 + 2 * i + m + 1],
                                       accum_out=stat[:, s0 + 2 * n + 2 * i + m:s0 + 2 * n + 2 * i + m + 1]
                                       ).then_inc(t_p, 1)
                return exp, keep

            def y_hi(b):
                act.wait_ge(w_tr, b + 1)
                m, c = b % 2, b // 2
                act.activation(yth3[:, 8 + 4 * c:12 + 4 * c, m * P:(m + 1) * P],
                               tb[2 + m][:, :].rearrange("p (k t) -> p k t", t=P), ACT.Copy).then_inc(w_hi, 1)

            h_exp, h_keep = heads(0, HEADS, sb1, pt1, 136, [tb[2], tb[2]])
            for j in range(1, 4):
                kvq_keep(j - 1)
                hi(U_KVQ + 2 * j + 2)
                hi(U_KVQ + 2 * j + 3)
            h_exp(0)
            h_keep(0)
            h_exp(1)
            kvq_keep(3)
            hi(U_KVQ + 10)
            h_keep(1)
            h_exp(2)
            h_keep(2)
            h_exp(3)
            hi(U_KVQ + 11)
            h_keep(3)
            h_exp(4)
            h_keep(4)
            h_exp(5)
            kvq_keep(4)
            h_keep(5)
            h_exp(6)
            hi(U_KVQ + 12)
            h_keep(6)
            h_exp(7)
            hi(U_KVQ + 13)
            h_keep(7)
            kvq_keep(5)
            y_hi(0)
            y_hi(1)
            for i in range(8, HEADS):
                if i > 8:
                    h_keep(i - 1)
                h_exp(i)
                if i == 8:
                    hi(U_WO + 2)
            h_keep(HEADS - 1)
            y_hi(2)
            y_hi(3)
            hi(U_WO + 3)
            hi(U_WO + 4)
            hi(U_WO + 5)
            norm(3)
            glu(1, U_GLU1, C_GLU1, 3, PAIR_GLU1)

            for m in range(M):
                square(FIN1, m, n_add, 4 * 3 + 2 * m + 2)
            norm(4)
            for m in range(M):
                square(5, m, f_app, m + 1)

            for l in range(2):
                U0, C0, k = gu(l), gc(l), 4 + 2 * l
                r, pair = STATS[k], pair_mix(l)
                if l == 1:
                    norm(6)
                act.wait_ge(x_ld, 48 * (l + 1))
                act.activation(ginh[:, :], gin[:, :], ACT.Copy).then_inc(x_gh, 1)
                hi(U0 + 2)
                hi(U0 + 3)
                act.wait_ge(n_r, r + 1)
                for m in range(M):
                    wait_group(act, C0, U0 + 2, m)
                    act.activation(sgc[:, m, :], pair_bank(pair, m)[:, 256:512], ACT.Sigmoid,
                                   scale=rms(r, m)).then_inc(x_sig, 1)
                act.wait_ge(x_g16, l + 1)
                for m in range(M):
                    act.activation(g16[:, m, :], tb[0][:, RANK * m:RANK * m + RANK], ACT.Copy,
                                   scale=rms(r, m)).then_inc(x_g16c, 1)
                hi(U0 + 4)
                act.wait_ge(x_gT, l + 1)
                act.activation(gT[0:RANK, :], tb[2][0:RANK, 0:SEQ], ACT.Copy).then_inc(x_gTc, 1)
                act.wait_ge(x_ctr, l + 1)
                act.wait_ge(x_pad, l + 1)
                act.activation(hpad[:, :, TAPS - 1:TAPS - 1 + SEQ], tb[1][:, :].rearrange("p (a t) -> p a t", t=SEQ),
                               ACT.Copy).then_inc(x_cpad, 1)
                hi(U0 + 5)
                act.wait_ge(x_lg, l + 1)
                tm = tmp[:, :, :].rearrange("p m c -> p (m c)")
                act.activation(tm, tb[3][:, :], ACT.Abs).then_inc(x_ab, 1)
                act.wait_ge(x_ab, l + 1)
                act.activation(tm, tm, ACT.Exp, scale=-1.0).then_inc(x_ex, 1)
                act.wait_ge(x_ex, l + 1)
                act.activation(tm, tm, ACT.Ln, bias=ones[:, 0:1]).then_inc(x_ln, 1)

                def keep(j, dst, n=512, func=ACT.Copy, tiles=range(M)):
                    for m in tiles:
                        wait_group(act, C0 + j, U0 + MIX_END[j], m)
                        act.activation(dst[:, m, :], pair_bank(j + pair, m)[:, 0:n], func,
                                       scale=rms(r, m)).then_inc(x_ev, 1)

                act.wait_ge(n_lo, 4 * k + 4)
                keep(1, gqk)
                hi(U0 + 6)
                act.wait_ge(x_cs, l + 1)
                act.wait_ge(n_sq, 2 * r + 2)
                flat = [z[:, :, :].rearrange("p a t -> p (a t)") for z in (gG, eG, nG, dG)]
                act.activation(flat[0], tb[3][:, :], ACT.Copy).then_inc(x_G, 1)
                act.activation(flat[1], tb[3][:, :], ACT.Exp, scale=1.0 / TAU).then_inc(x_e1, 1)
                act.activation(flat[2], tb[3][:, :], ACT.Exp, scale=-1.0 / TAU).then_inc(x_e1, 1)
                hi(U0 + 7)
                act.wait_ge(x_gd, l + 1)
                act.activation(flat[3], flat[3], ACT.Exp, scale=1.0 / TAU).then_inc(x_e2, 1)
                keep(2, gv)
                hi(U0 + 8)
                act.wait_ge(x_kdtr, l + 1)
                act.activation(kdt[:, :, :].rearrange("p m c -> p (m c)"), tb[0][:, :], ACT.Copy).then_inc(x_kdc, 1)
                hi(U0 + 9)
                keep(3, mqk)
                hi(U0 + 10)
                act.wait_ge(x_mtr, 2 * l + 1)
                act.activation(mqT[:, :, :].rearrange("p a t -> p (a t)"), tb[1][:, :], ACT.Copy).then_inc(x_mcp, 1)
                act.wait_ge(x_mtr, 2 * l + 2)
                act.activation(mkT[:, :, :].rearrange("p a t -> p (a t)"), tb[2][:, :], ACT.Copy).then_inc(x_mcp, 1)
                keep(4, mv, 256)
                hi(U0 + 11)
                h_exp, h_keep = heads(HEADS + 4 * l, 4, sb2, pt2, 232 + 24 * l, [tb[1], tb[1]])
                h_exp(0)

                def o_keep(b):
                    act.wait_ge(x_o, 2 * l + b + 1)
                    act.activation(og[:, :, :].rearrange("p m (a b d) -> p b (m a) d", b=2, d=DV)[:, b, :, :],
                                   tb[0][:, :].rearrange("p (c d) -> p c d", d=DV), ACT.Copy).then_inc(x_oc, 1)

                o_keep(0)
                h_keep(0)
                hi(U0 + 12)
                act.wait_ge(x_btr, l + 1)
                for a in range(2):
                    act.activation(ycs[:, a, :], tb[3][:, a * SEQ:(a + 1) * SEQ], ACT.Silu, scale=cln[:, l, a, 0:1],
                                   bias=cln[:, l, a, 1:2]).then_inc(x_sl, 1)
                o_keep(1)
                act.wait_ge(x_sl, 2 * l + 2)
                act.activation(yth[:, 0:512], ycs[:, :, :].rearrange("p a t -> p (a t)"), ACT.Copy).then_inc(x_yh, 1)
                keep(5, rs, 512, ACT.Silu, (0,))
                h_exp(1)
                keep(5, rs, 512, ACT.Silu, (1,))
                h_keep(1)
                h_exp(2)
                for m in range(M):
                    act.wait_ge(x_yg, 3 * l + 1 + m)
                    act.activation(yth3[:, 4:8, m * P:(m + 1) * P], xg[:, 1 + m, :].rearrange("p (k t) -> p k t", t=P),
                                   ACT.Copy).then_inc(x_yh, 1)
                h_keep(2)
                h_exp(3)
                hi(U0 + 13)
                h_keep(3)
                hi(U0 + 14)
                hi(U0 + 15)
                act.wait_ge(x_yg, 3 * l + 3)
                act.activation(yth[:, 512:1024], xg[:, 0, :], ACT.Copy).then_inc(x_yh, 1)
                hi(U0 + 16)
                norm(k + 1)

                U1, C1, r1 = U0 + 15, C0 + 6, STATS[k + 1]

                def up_keep(j, t=0):
                    for m in range(M):
                        wait_group(act, C1 + j, U1 + 2 * j + 2, m, t)
                        if j == 0 and m == 0:
                            act.wait_ge(n_r, r1 + 1)
                        act.activation(us[:, j % 2, m, :], pair_bank(j + pair, m)[:, :], ACT.Copy,
                                       scale=rms(r1, m)).then_inc(f_ev, 1)

                def tap2(j, t=0):
                    act.wait_ge(f_tr, CTF * l + j + 1 + 2 * t)
                    if j >= 2:
                        act.wait_ge(f_pr, CTF * l + j - 1 + 2 * t)
                    for a in range(4):
                        c = 16 * j + 4 * a
                        o = act.activation(cv[:, j % 2, a, :], tb[2 * (j % 2) + a // 2][:, (a % 2) * SEQ:(a % 2 + 1) * SEQ],
                                           ACT.Identity, scale=fcw[:, l, bass.ds(c + 2 + 32 * t, 1)],
                                           bias=fcw[:, l, bass.ds(c + 3 + 32 * t, 1)])
                    o.then_inc(f_t0, 1)

                def fsilu(j, t=0):
                    act.wait_ge(f_t2, CTF * l + j + 1 + 2 * t)
                    act.activation(cv[:, j % 2, 0:2, :], cv[:, j % 2, 0:2, :], ACT.Silu).then_inc(f_si, 1)

                def fhi(j, t=0):
                    act.wait_ge(f_pr, CTF * l + j + 1 + 2 * t)
                    act.activation(yth[:, bass.ds((2 * j + 4 * t) * SEQ, 512)],
                                   pr[:, j % 2, :, :].rearrange("p a t -> p (a t)"), ACT.Copy).then_inc(f_hi, 1)

                def fstep(j, t=0):
                    up_keep(j - 1, t)
                    hi(U1 + 2 * j + 2, t)
                    if j >= 2:
                        fsilu(j - 2, t)
                    hi(U1 + 2 * j + 3, t)
                    if j >= 2:
                        fhi(j - 2, t)
                    tap2(j - 1, t)

                hi(U1 + 2)
                hi(U1 + 3)
                fstep(1)
                fstep(2)
                with act.Fori(0, (CTF - 3) // 2) as t:
                    fstep(3, t)
                    fstep(4, t)
                up_keep(CTF - 1)
                hi(U1 + 2 * CTF + 2)
                fsilu(CTF - 2)
                fhi(CTF - 2)
                tap2(CTF - 1)
                fsilu(CTF - 1)
                hi(U1 + 2 * CTF + 3)
                fhi(CTF - 1)
                for j in range(2, CTF):
                    hi(U1 + 2 * CTF + j + 2)
            for m in range(M):
                square(FIN2, m, n_add, 4 * 7 + 2 * m + 2)

        @block.vector
        def _(dve):
            def lo(U, t=0):
                if U >= TOTAL:
                    return
                s = U % SLOTS
                dve.wait_ge(hi_ready, U + 1 + 4 * t)
                dve.tensor_tensor(wlo[:, s, :], raw[:, s, :], whi[:, s, :], ALU.subtract).then_inc(lo_ready, 1)

            def add(k, q):
                m, c = divmod(q, 2)
                wait_out(dve, k, OUT_END[k], q)
                xs = x[:, m, 512 * c:512 * c + 512]
                dve.tensor_tensor(xs, out_bank(OUT_PAIR[k], m, c)[:, :], xs, ALU.add).then_inc(n_add, 1)

            def gain(q, g, dst):
                c = q % 2
                return dve.tensor_tensor(dst[:, q, :].rearrange("p (k t) -> p k t", t=P),
                                         tb[q][:, :].rearrange("p (k t) -> p k t", t=P),
                                         gcol[:, g, 4 * c:4 * c + 4].unsqueeze(2).to_broadcast([P, 4, P]), ALU.mult)

            def norm_gain(k, q):
                dve.wait_ge(n_tr, 4 * k + q + 1)
                gain(q, 8 if k == 7 else k, xg0 if k == 0 else xg).then_inc(n_gm, 1)

            def norm_lo(k, q):
                m, c = divmod(q, 2)
                s = slice(4 * c, 4 * c + 4), slice(m * P, (m + 1) * P)
                dve.wait_ge(n_hi, 4 * k + q + 1)
                dve.tensor_tensor(xtl[:, s[0], s[1]],
                                  (xg0 if k == 0 else xg)[:, q, :].rearrange("p (k t) -> p k t", t=P),
                                  xth[:, s[0], s[1]], ALU.subtract).then_inc(n_lo, 1)

            def norm(k):
                add(k, 0)
                add(k, 1)
                norm_gain(k, 0)
                add(k, 2)
                norm_lo(k, 0)
                add(k, 3)
                norm_gain(k, 1)
                norm_lo(k, 1)
                norm_gain(k, 2)
                norm_gain(k, 3)
                norm_lo(k, 2)
                norm_lo(k, 3)

            dve.wait_ge(gains_loaded, 16)
            norm_gain(0, 0)
            norm_gain(0, 1)
            norm_lo(0, 0)
            norm_lo(0, 1)
            lo(0)
            lo(1)
            norm_gain(0, 2)
            norm_gain(0, 3)
            norm_lo(0, 2)
            norm_lo(0, 3)

            def gate(jj):
                for m in range(M):
                    dve.wait_ge(a_ev, 8 + 2 * jj + m + 1)
                    dve.wait_ge(a_spc, 4 * m + jj + 1)
                    for g in range(2):
                        c = 512 * jj + 256 * g
                        u = ug[:, jj % 2, m, 256 * g:256 * g + 256]
                        o = dve.scalar_tensor_tensor(u, v_a[:, m, c:c + 256], bsc[:, 2 * jj + g:2 * jj + g + 1], u,
                                                     ALU.add, ALU.mult)
                    o.then_inc(a_y, 1)

            def gate_lo(jj):
                for m in range(M):
                    s = slice(4 * jj, 4 * jj + 4), slice(m * P, (m + 1) * P)
                    dve.wait_ge(a_hi, 2 * jj + m + 1)
                    dve.tensor_tensor(ytl3[:, s[0], s[1]], tb[2 * (jj % 2) + m][:, :].rearrange("p (k t) -> p k t", t=P),
                                      yth3[:, s[0], s[1]], ALU.subtract).then_inc(a_lo, 1)

            lo(2)
            lo(3)
            for j in range(1, 8):
                if j == 4:
                    dve.wait_ge(a_vsq, 8)
                    dve.tensor_reduce(stat[:, 64:66], stat[:, 128:136].rearrange("p (m j) -> p m j", j=4), AX.X,
                                      ALU.add).then_inc(a_vsum, 1)
                lo(2 * j + 2)
                lo(2 * j + 3)
                if j == 4:
                    dve.wait_ge(a_r, 1)
                    dve.wait_ge(consts_loaded, 16 * 8)
                    for m in range(M):
                        dve.scalar_tensor_tensor(v_a[:, m, :], v_a[:, m, :], stat[:, 68 + m:69 + m], gs_sb[:, :],
                                                 ALU.mult, ALU.mult).then_inc(a_vn, 1)
                if j >= 5:
                    gate(j - 5)
                if j == 6:
                    gate_lo(0)
                if j == 7:
                    gate_lo(1)
                    gate_lo(2)
            for j in range(8):
                if j == 0:
                    gate(3)
                lo(U_OUTA + j + 2)
                if j == 0:
                    gate_lo(3)
            norm(1)

            def glu(e, U0, k, pair):
                def gated(j, t=0):
                    for m in range(M):
                        dve.wait_ge(g_silu, 2 * CTF * e + 2 * j + m + 1 + 4 * t)
                        dve.scalar_tensor_tensor(yy[:, j % 2, m, :], pair_bank(j + pair, m)[:, 256:512], rms(STATS[k], m),
                                                 sg[:, j % 2, m, :], ALU.mult, ALU.mult).then_inc(g_mul, 1)

                def keep(j, t=0):
                    dve.wait_ge(g_hi, CTF * e + j + 1 + 2 * t)
                    s = bass.ds((2 * j + 4 * t) * SEQ, 512)
                    dve.tensor_tensor(ytl[:, s], tb[j % 2][:, :], yth[:, s], ALU.subtract).then_inc(g_lo, 1)

                lo(U0 + 2)
                lo(U0 + 3)
                for j in (1, 2):
                    gated(j - 1)
                    lo(U0 + 2 * j + 2)
                    lo(U0 + 2 * j + 3)
                    keep(j - 1)
                with dve.Fori(0, (CTF - 3) // 2) as t:
                    for j in (3, 4):
                        gated(j - 1, t)
                        lo(U0 + 2 * j + 2, t)
                        lo(U0 + 2 * j + 3, t)
                        keep(j - 1, t)
                gated(CTF - 1)
                lo(U0 + 2 * CTF + 2)
                keep(CTF - 1)
                for j in range(1, CTF):
                    lo(U0 + 2 * CTF + j + 2)

            glu(0, U_GLU0, 1, PAIR_GLU0)
            norm(2)
            for q in range(4):
                if q == 0:
                    dve.wait_ge(n_lo, 12)
                gain(q, 7, xg).then_inc(q_gm, 1)
            lo(U_KVQ + 2)
            lo(U_KVQ + 3)
            for q in range(4):
                m, c = divmod(q, 2)
                s = slice(4 * c, 4 * c + 4), slice(m * P, (m + 1) * P)
                dve.wait_ge(q_hi, q + 1)
                dve.tensor_tensor(ytl3[:, s[0], s[1]], xg[:, q, :].rearrange("p (k t) -> p k t", t=P),
                                  yth3[:, s[0], s[1]], ALU.subtract).then_inc(q_lo, 1)

            def kq_copy(i, m):
                dst, c = (qT, kT)[i % 2 == 0], i // 2
                dve.wait_ge(k_tr, 2 * i + m + 1)
                dve.tensor_copy(dst[:, 4 * c:4 * c + 4, m * P:(m + 1) * P],
                                KQ_BANK[i][m][:, :].rearrange("p (k t) -> p k t", t=P)).then_inc(k_cp, 1)

            def heads(h0, n, sb, s0, bias, dst, s_banks, o_banks):
                scale = float(DH) ** -0.5

                def finish(i):
                    h = h0 + i
                    dve.wait_ge(t_p, 2 * h + 2)
                    rd = stat[:, s0 + 4 * n + 2 * i:s0 + 4 * n + 2 * i + 2]
                    dve.reciprocal(rd, stat[:, s0 + 2 * n + 2 * i:s0 + 2 * n + 2 * i + 2]).then_inc(t_rd, 1)
                    dve.wait_ge(t_rd, h + 1)
                    dve.wait_ge(t_o, h + 1)
                    dve.tensor_tensor(dst(i), o_banks[i % 2].rearrange("p (m d) -> p m d", d=DH),
                                      rd.unsqueeze(2).to_broadcast([P, M, DH]), ALU.mult).then_inc(t_on, 1)

                def begin(i):
                    h = h0 + i
                    dve.wait_ge(t_s, h + 1)
                    if i >= 2:
                        dve.wait_ge(t_pt, h - 1)
                    b = bias(i)
                    dve.scalar_tensor_tensor(sb[:, i % 2, 0:P], s_banks[i % 2][:, 0:P], scale, b[:, P:2 * P],
                                             ALU.mult, ALU.add)
                    dve.scalar_tensor_tensor(sb[:, i % 2, P:3 * P], s_banks[i % 2][:, P:3 * P], scale, b,
                                             ALU.mult, ALU.add).then_inc(t_sb, 1)
                    dve.wait_ge(t_sb, h + 1)
                    for m, w in enumerate((sb[:, i % 2, 0:P], sb[:, i % 2, P:3 * P])):
                        dve.tensor_reduce(stat[:, s0 + 2 * i + m:s0 + 2 * i + m + 1], w, AX.X, ALU.max,
                                          negate=True).then_inc(t_mx, 1)

                return begin, finish

            def rel(i):
                dve.wait_ge(rb_ok, i // 2 + 1)
                return rb[:, (i // 2) % 2, i % 2, :]

            qTo = qT[:, :, :].rearrange("p c (m d) -> p c m d", d=P)
            def y_lo(b):
                m, c = b % 2, b // 2
                s = slice(8 + 4 * c, 12 + 4 * c), slice(m * P, (m + 1) * P)
                dve.wait_ge(w_hi, b + 1)
                dve.tensor_tensor(ytl3[:, s[0], s[1]], tb[2 + m][:, :].rearrange("p (k t) -> p k t", t=P),
                                  yth3[:, s[0], s[1]], ALU.subtract).then_inc(w_lo, 1)

            begin, finish = heads(0, HEADS, sb1, 136, rel,
                                  lambda i: qTo[:, i // 2, :, DH * (i % 2):DH * (i % 2) + DH],
                                  tb[0:2], [tb[0][:, 384:512], tb[1][:, 384:512]])
            lo(U_KVQ + 4)
            lo(U_KVQ + 5)
            kq_copy(0, 0)
            kq_copy(0, 1)
            lo(U_KVQ + 6)
            lo(U_KVQ + 7)
            lo(U_KVQ + 8)
            kq_copy(1, 0)
            kq_copy(1, 1)
            begin(0)
            lo(U_KVQ + 9)
            begin(1)
            finish(0)
            lo(U_KVQ + 10)
            begin(2)
            finish(1)
            kq_copy(2, 0)
            begin(3)
            finish(2)
            kq_copy(2, 1)
            lo(U_KVQ + 11)
            begin(4)
            finish(3)
            begin(5)
            finish(4)
            begin(6)
            finish(5)
            lo(U_KVQ + 12)
            begin(7)
            finish(6)
            lo(U_KVQ + 13)
            finish(7)
            kq_copy(3, 0)
            kq_copy(3, 1)
            y_lo(0)
            y_lo(1)
            for i in range(8, HEADS):
                begin(i)
                if i > 8:
                    finish(i - 1)
                if i == 9:
                    lo(U_WO + 2)
            finish(HEADS - 1)
            y_lo(2)
            y_lo(3)
            lo(U_WO + 3)
            lo(U_WO + 4)
            lo(U_WO + 5)
            norm(3)
            glu(1, U_GLU1, 3, PAIR_GLU1)

            def apply(r, e, m):
                if m == 0:
                    dve.wait_ge(f_rt, e + 1)
                    dve.wait_ge(f_row, 16 * (e + 1))
                else:
                    dve.wait_ge(n_r, r + 1)
                dve.scalar_tensor_tensor(x[:, m, :], x[:, m, :], rms(r, m), frow[:, :], ALU.mult,
                                         ALU.mult).then_inc(f_app, 1)

            add(4, 0)
            add(4, 1)
            add(4, 2)
            apply(FIN1, 0, 0)
            add(4, 3)
            norm_gain(4, 0)
            norm_gain(4, 1)
            norm_lo(4, 0)
            norm_lo(4, 1)
            apply(FIN1, 0, 1)
            norm_gain(4, 2)
            norm_gain(4, 3)
            norm_lo(4, 2)
            norm_lo(4, 3)

            for l in range(2):
                U0, k = gu(l), 4 + 2 * l
                r, pair = STATS[k], pair_mix(l)
                if l == 1:
                    norm(6)
                dve.wait_ge(x_gh, l + 1)
                dve.tensor_tensor(ginl[:, :], gin[:, :], ginh[:, :], ALU.subtract).then_inc(x_gl, 1)
                lo(U0 + 2)
                lo(U0 + 3)
                for m in range(M):
                    dve.wait_ge(x_sig, 2 * l + m + 1)
                    dve.scalar_tensor_tensor(hc[:, m, :], pair_bank(pair, m)[:, 0:256], rms(r, m), sgc[:, m, :],
                                             ALU.mult, ALU.mult).then_inc(x_gated, 1)
                lo(U0 + 4)
                lo(U0 + 5)

                first = [(0, i) for i in range(TAPS)]
                second = [(1, i) for i in range(POOL_TAPS, TAPS)]
                order = []
                while first:
                    order += [first.pop(0)] + ([second.pop(0)] if second else [])

                def taps(n0, n1):
                    for a, i in order[n0:n1]:
                        src = hpad[:, a, i:i + SEQ]
                        w = cw[:, l, a, i:i + 1]
                        i0, done, n = (0, x_tap, TAPS) if a == 0 else (POOL_TAPS, x_tap1, TAPS - POOL_TAPS + 1)
                        if i == i0:
                            dve.tensor_scalar(cacc[:, a, :], src, w, cw[:, l, a, TAPS:TAPS + 1], ALU.mult,
                                              ALU.add).then_inc(done, 1)
                        else:
                            dve.wait_ge(done, n * l + i - i0)
                            dve.scalar_tensor_tensor(cacc[:, a, :], src, w, cacc[:, a, :], ALU.mult,
                                                     ALU.add).then_inc(done, 1)

                dve.wait_ge(x_cpad, l + 1)
                taps(0, 9)
                dve.wait_ge(x_ln, l + 1)
                dve.scalar_tensor_tensor(la[:, :, :].rearrange("p m c -> p (m c)"), tb[3][:, :], 0.0,
                                         tmp[:, :, :].rearrange("p m c -> p (m c)"), ALU.min,
                                         ALU.subtract).then_inc(x_la, 1)
                taps(9, 14)
                lo(U0 + 6)
                dve.wait_ge(x_G, l + 1)
                g4 = gG[:, :, :].rearrange("p a (n c) -> p (a n) c", c=GCH)
                d4 = dG[:, :, :].rearrange("p a (n c) -> p (a n) c", c=GCH)
                dve.tensor_tensor(d4, g4[:, :, GCH - 1:GCH].to_broadcast([P, 2 * NCH, GCH]), g4,
                                  ALU.subtract).then_inc(x_gd, 1)
                dve.wait_ge(x_e1, 2 * l + 2)
                e4 = eG[:, :, :].rearrange("p a (n c) -> p a n c", c=GCH)
                dve.tensor_copy(dec[:, :, :], e4[:, :, :, GCH - 1]).then_inc(x_qg, 1)
                dve.wait_ge(x_qktr, 2 * l + 2)
                dve.wait_ge(x_qg, 3 * l + 1)
                ef, nf, df = (z[:, :, :].rearrange("p a t -> p (a t)") for z in (eG, nG, dG))
                dve.scalar_tensor_tensor(ef, tb[1][:, :], float(DK) ** -0.5, ef, ALU.mult, ALU.mult).then_inc(x_qg, 1)
                dve.tensor_tensor(nf, tb[2][:, :], nf, ALU.mult).then_inc(x_qg, 1)
                taps(14, 17)
                lo(U0 + 7)
                dve.wait_ge(x_e2, l + 1)
                dve.tensor_tensor(df, tb[2][:, :], df, ALU.mult).then_inc(x_kd, 1)
                taps(17, 24)
                lo(U0 + 8)
                dve.wait_ge(x_at0, l + 1)
                for b in range(2):
                    dve.wait_ge(x_A, 2 * l + b + 1)
                    for c in range(0, 4 * P, P):
                        o = dve.copy_predicated(aT[:, b, c:c + P], tri[:, :].bitcast(U32), tb[1 + b][:, c:c + P])
                    o.then_inc(x_Am, 1)
                taps(24, 28)
                lo(U0 + 9)

                def state(n):
                    dve.wait_ge(x_dS, (NCH - 1) * l + n + 1)
                    if n:
                        dve.wait_ge(x_St, (NCH - 1) * l + n)
                    for a in range(2):
                        inc = tb[3 * (n % 2)][:, P * a:P * a + P]
                        if n == 0:
                            o = dve.tensor_copy(st_g[:, 0, a, :], inc)
                        else:
                            o = dve.scalar_tensor_tensor(st_g[:, n, a, :], st_g[:, n - 1, a, :], dec[:, a, n:n + 1],
                                                         inc, ALU.mult, ALU.add)
                    o.then_inc(x_St, 1)

                state(0)
                taps(28, 31)
                state(1)
                state(2)
                taps(31, 34)
                state(3)
                lo(U0 + 10)
                state(4)
                taps(34, 38)
                state(5)
                taps(38, 42)
                dve.wait_ge(x_pa, (POOL_TAPS - 1) * (l + 1))
                dve.wait_ge(x_tap1, (TAPS - POOL_TAPS + 1) * l + TAPS - POOL_TAPS)
                dve.tensor_tensor(cacc[:, 1, :], cacc[:, 1, :], cacc2[:, :], ALU.add).then_inc(x_tap1, 1)
                state(6)
                lo(U0 + 11)
                moc = mo[:, :, :].rearrange("p m (h d) -> p m h d", d=DH)
                begin, finish = heads(HEADS + 4 * l, 4, sb2, 232 + 24 * l, lambda i: cmask[:, :],
                                      lambda i: moc[:, :, i, :], tb[2:4], [tb[2][:, 384:512], tb[3][:, 384:512]])
                begin(0)
                for m in range(M):
                    dve.wait_ge(x_ltr, l + 1)
                    dve.bn_stats(bnst[:, m, 0:6], tb[3][:, m * 256:(m + 1) * 256]).then_inc(x_bn, 1)
                    dve.wait_ge(x_bn, 2 * l + m + 1)
                    dve.bn_aggr(mvv[:, m, :], bnst[:, m, 0:6]).then_inc(x_ag, 1)
                dve.wait_ge(x_lr, l + 1)
                for m in range(M):
                    dve.tensor_scalar(cvn[:, m, :], tb[3][:, m * 256:(m + 1) * 256], mvv[:, m, 0:1],
                                      stat[:, 74 + m:75 + m], ALU.subtract, ALU.mult).then_inc(x_nrm, 1)
                lo(U0 + 12)
                ogf = og[:, :, :].rearrange("p m c -> p (m c)")
                dve.wait_ge(x_oc, 2 * l + 2)
                dve.tensor_tensor(osq[:, :, :].rearrange("p m c -> p (m c)"), ogf, ogf, ALU.mult).then_inc(x_osq, 1)
                dve.wait_ge(x_osq, 2 * l + 1)
                dve.tensor_reduce(stat[:, 96:104], osq[:, :, :].rearrange("p m (h d) -> p (m h) d", d=DV), AX.X,
                                  ALU.add).then_inc(x_oss, 1)
                dve.wait_ge(x_yh, 4 * l + 1)
                dve.tensor_tensor(ytl[:, 0:512], ycs[:, :, :].rearrange("p a t -> p (a t)"), yth[:, 0:512],
                                  ALU.subtract).then_inc(x_yl, 1)
                finish(0)
                begin(1)
                begin(2)
                dve.wait_ge(x_or, 2 * l + 1)
                for m in range(M):
                    dve.wait_ge(x_ev, 10 * l + 9 + m)
                    for h in range(GH):
                        o = og[:, m, h * DV:(h + 1) * DV]
                        last = dve.scalar_tensor_tensor(o, o, stat[:, 112 + GH * m + h:113 + GH * m + h],
                                                        rs[:, m, h * DV:(h + 1) * DV], ALU.mult, ALU.mult)
                    last.then_inc(x_on2, 1)
                finish(1)
                for m in range(M):
                    dve.wait_ge(x_ytr, 3 * l + 1 + m)
                    dve.tensor_tensor(xg[:, 1 + m, :].rearrange("p (k t) -> p k t", t=P),
                                      tb[0][:, :].rearrange("p (k t) -> p k t", t=P),
                                      glg[:, l, :].unsqueeze(2).to_broadcast([P, 4, P]), ALU.mult).then_inc(x_yg, 1)
                for m in range(M):
                    s = slice(4, 8), slice(m * P, (m + 1) * P)
                    dve.wait_ge(x_yh, 4 * l + 2 + m)
                    dve.tensor_tensor(ytl3[:, s[0], s[1]], xg[:, 1 + m, :].rearrange("p (k t) -> p k t", t=P),
                                      yth3[:, s[0], s[1]], ALU.subtract).then_inc(x_yl, 1)
                begin(3)
                lo(U0 + 13)
                finish(2)
                finish(3)
                mof = mo[:, :, :].rearrange("p m c -> p (m c)")
                dve.wait_ge(t_on, HEADS + 4 * l + 4)
                dve.wait_ge(x_yg, 3 * l + 2)
                dve.tensor_tensor(msq[:, :, :].rearrange("p m c -> p (m c)"), mof, mof, ALU.mult).then_inc(x_osq, 1)
                dve.wait_ge(x_osq, 2 * l + 2)
                dve.tensor_reduce(stat[:, 104:112], msq[:, :, :].rearrange("p m (h d) -> p (m h) d", d=DH), AX.X,
                                  ALU.add).then_inc(x_oss, 1)
                lo(U0 + 14)
                dve.wait_ge(x_or, 2 * l + 2)
                m3 = mo[:, :, :].rearrange("p m (h d) -> p (m h) d", d=DH)
                dve.tensor_tensor(m3, m3, stat[:, 120:128].unsqueeze(2).to_broadcast([P, 8, DH]),
                                  ALU.mult).then_inc(x_on, 1)
                dve.wait_ge(x_ytr, 3 * l + 3)
                dve.tensor_tensor(xg[:, 0, :].rearrange("p (a t) -> p a t", t=SEQ),
                                  tb[0][:, :].rearrange("p (a t) -> p a t", t=SEQ),
                                  mog[:, l, :].unsqueeze(2).to_broadcast([P, 2, SEQ]), ALU.mult).then_inc(x_yg, 1)
                dve.wait_ge(x_yh, 4 * l + 4)
                dve.tensor_tensor(ytl[:, 512:1024], xg[:, 0, :], yth[:, 512:1024], ALU.subtract).then_inc(x_yl, 1)
                lo(U0 + 15)
                lo(U0 + 16)
                norm(k + 1)

                U1 = U0 + 15

                def taps10(j, t=0):
                    dve.wait_ge(f_t0, CTF * l + j + 1 + 2 * t)
                    for tap, s in ((1, f_t1), (0, f_t2)):
                        back = 2 - tap
                        for a in range(4):
                            src = tb[2 * (j % 2) + a // 2][:, (a % 2) * SEQ:(a % 2 + 1) * SEQ - back]
                            dst = cv[:, j % 2, a, back:SEQ]
                            o = dve.scalar_tensor_tensor(dst, src, fcw[:, l, bass.ds(16 * j + 4 * a + tap + 32 * t, 1)],
                                                         dst, ALU.mult, ALU.add)
                        o.then_inc(s, 1)
                        if tap:
                            dve.wait_ge(f_t1, CTF * l + j + 1 + 2 * t)

                def product(j, t=0):
                    dve.wait_ge(f_si, CTF * l + j + 1 + 2 * t)
                    dve.tensor_tensor(pr[:, j % 2, :, :], cv[:, j % 2, 0:2, :], cv[:, j % 2, 2:4, :],
                                      ALU.mult).then_inc(f_pr, 1)

                def flo(j, t=0):
                    dve.wait_ge(f_hi, CTF * l + j + 1 + 2 * t)
                    s = bass.ds((2 * j + 4 * t) * SEQ, 512)
                    dve.tensor_tensor(ytl[:, s], pr[:, j % 2, :, :].rearrange("p a t -> p (a t)"), yth[:, s],
                                      ALU.subtract).then_inc(f_lo, 1)

                def fstep(j, t=0):
                    lo(U1 + 2 * j + 2, t)
                    if j >= 2:
                        product(j - 2, t)
                    lo(U1 + 2 * j + 3, t)
                    if j >= 2:
                        flo(j - 2, t)
                    taps10(j - 1, t)

                lo(U1 + 2)
                lo(U1 + 3)
                fstep(1)
                fstep(2)
                with dve.Fori(0, (CTF - 3) // 2) as t:
                    fstep(3, t)
                    fstep(4, t)
                lo(U1 + 2 * CTF + 2)
                product(CTF - 2)
                flo(CTF - 2)
                taps10(CTF - 1)
                product(CTF - 1)
                lo(U1 + 2 * CTF + 3)
                flo(CTF - 1)
                for j in range(2, CTF):
                    lo(U1 + 2 * CTF + j + 2)
            for q in range(3):
                add(8, q)
            apply(FIN2, 1, 0)
            add(8, 3)
            apply(FIN2, 1, 1)

        @block.tensor
        def _(pe):
            def split3(o, xh, xl, wh, wl, first, last):
                pe.matmul(o, xh, wh, start=first, stop=False)
                pe.matmul(o, xh, wl, start=False, stop=False)
                return pe.matmul(o, xl, wh, start=False, stop=last)

            def in_group(o, m, U, t=0, a=xth, b=xtl, norm=None, count=0, mid=None, hooks={}):
                for half in range(2):
                    s = (U + half) % SLOTS
                    if m == 0:
                        pe.wait_ge(lo_ready, U + half + 1 + 4 * t)
                    if norm is not None:
                        pe.wait_ge(norm, count + 2 * m + half + 1)
                    for kk in range(4):
                        kt = 4 * half + kk
                        ts = slice(m * P, (m + 1) * P)
                        ws = slice(512 * kk, 512 * kk + 512)
                        mm = split3(o, a[:, kt, ts], b[:, kt, ts], whi[:, s, ws], wlo[:, s, ws], kt == 0, kt == KT - 1)
                        if kt == 1 and mid is not None:
                            mid()
                        if kt in hooks:
                            hooks[kt]()
                    if m == 1 and half == 0:
                        mm.then_inc(unit_used, 1)
                mm.then_inc(m0_done if m == 0 else unit_used, 1)

            def turn(o, i, n=P):
                return pe.transpose(o, i, ident[0:n, 0:n])

            def norm_turn(k, q, after=None, count=0):
                m, c = divmod(q, 2)
                if after is not None:
                    pe.wait_ge(after, count)
                for i in range(4):
                    mm = turn(tb[q][:, i * P:(i + 1) * P], x[:, m, 512 * c + i * P:512 * c + (i + 1) * P])
                mm.then_inc(n_tr, 1)

            def out_product(k, U, n, pair, y0, ready, between=None, order=None, hooks={}):
                for j in range(n):
                    s = (U + j) % SLOTS
                    pe.wait_ge(lo_ready, U + j + 1)
                    ready(j)
                    for q in range(4):
                        m, c = divmod(q, 2)
                        if j == 0:
                            ready(("bank", m))
                        for kk in range(2):
                            kt = y0 + 2 * (order[j] if order else j) + kk
                            ts = slice(m * P, (m + 1) * P)
                            ws = slice(1024 * kk + 512 * c, 1024 * kk + 512 * c + 512)
                            mm = split3(out_bank(pair, m, c)[:, :], yth3[:, kt, ts], ytl3[:, kt, ts], whi[:, s, ws],
                                        wlo[:, s, ws], j == 0 and kk == 0, j == n - 1 and kk == 1)
                        if q == 3:
                            mm.then_inc(unit_used, 1)
                        elif j == n - 1:
                            mm.then_inc(out_group, 1)
                        if (j, q) in hooks:
                            hooks[j, q]()
                        if j == n - 1 and k not in (4, 8):
                            if q == 2:
                                norm_turn(k, 0, n_add, 4 * (k - 1) + 1)
                            if q == 3:
                                norm_turn(k, 1, n_add, 4 * (k - 1) + 2)
                                norm_turn(k, 2, n_add, 4 * (k - 1) + 3)
                    if between is not None:
                        between(j)

            def last_turn(k):
                return lambda: norm_turn(k, 3, n_add, 4 * (k - 1) + 4)

            pe.wait_ge(consts_made, 1)
            for q in range(2):
                norm_turn(0, q, x_loaded[0], 16)

            def second_tokens():
                for q in (2, 3):
                    norm_turn(0, q, x_loaded[1], 16)

            def spatial(m):
                if m == 0:
                    pe.wait_ge(a_vn, 2)
                    pe.wait_ge(consts_made, 4)
                for b in range(4):
                    if m == 1:
                        pe.wait_ge(a_spc, b + 1)
                    for g in (2 * b, 2 * b + 1):
                        mm = pe.matmul(tb[b][:, (g % 2) * GDIM:(g % 2 + 1) * GDIM], ws_sb[:, g, :],
                                       v_a[:, m, g * GDIM:(g + 1) * GDIM], start=True, stop=True)
                    mm.then_inc(a_sp, 1)

            def gmlp_turn(jj):
                for m in range(M):
                    pe.wait_ge(a_y, 2 * jj + m + 1)
                    if jj < 2:
                        pe.wait_ge(a_spc, 8)
                    else:
                        pe.wait_ge(a_lo, 2 * (jj - 2) + m + 1)
                    for i in range(4):
                        mm = turn(tb[2 * (jj % 2) + m][:, i * P:(i + 1) * P], ug[:, jj % 2, m, i * P:(i + 1) * P])
                    mm.then_inc(a_tr, 1)

            for j in range(8):
                for m in range(M):
                    if j >= 2:
                        pe.wait_ge(a_ev, 2 * (j - 2) + m + 1)
                    in_group(pair_bank(j + PAIR_IN, m)[:, :], m, U_IN + 2 * j, norm=n_lo if j == 0 else None,
                             hooks={3: (lambda m=m: spatial(m))} if j == 5 else
                             {1: second_tokens} if j == m == 0 else {})
                    if j == 6:
                        gmlp_turn(m)
                if j == 7:
                    gmlp_turn(2)

            def out_a_ready(j):
                if isinstance(j, tuple):
                    pe.wait_ge(a_ev, 14 + 2 * j[1] if j[1] == 0 else 16)
                elif j % 2 == 0:
                    pe.wait_ge(a_lo, 2 * (j // 2) + 2)

            out_product(1, U_OUTA, 8, PAIR_OUTA, 0, out_a_ready, lambda j: gmlp_turn(3) if j == 0 else None)

            def glu(e, U0, k, pair):
                def glu_turn(j, t=0):
                    pe.wait_ge(g_mul, 2 * CTF * e + 2 * j + 2 + 4 * t)
                    if j >= 2:
                        pe.wait_ge(g_lo, CTF * e + j - 1 + 2 * t)
                    for m in range(M):
                        for i in range(2):
                            mm = turn(tb[j % 2][:, i * SEQ + m * P:i * SEQ + (m + 1) * P],
                                      yy[:, j % 2, m, i * P:(i + 1) * P])
                    mm.then_inc(g_tr, 1)

                def step(j, t=0):
                    for m in range(M):
                        if j >= 2:
                            pe.wait_ge(g_mul, 2 * CTF * e + 2 * (j - 2) + m + 1 + 4 * t)
                        in_group(pair_bank(j + pair, m)[:, :], m, U0 + 2 * j, t, norm=n_lo if j == 0 else None,
                                 count=4 * k, mid=last_turn(k) if j == 0 and m == 0 else None)
                        if m == 0 and j >= 1:
                            glu_turn(j - 1, t)

                for j in range(3):
                    step(j)
                with pe.Fori(0, (CTF - 3) // 2) as t:
                    step(3, t)
                    step(4, t)
                return glu_turn

            def glu_ready(e):
                def ready(j):
                    if isinstance(j, tuple):
                        pe.wait_ge(g_mul, 2 * CTF * e + 2 * CTF - 2 * (1 - j[1]))
                    else:
                        pe.wait_ge(g_lo, CTF * e + j + 1)
                return ready

            turn0 = glu(0, U_GLU0, 1, PAIR_GLU0)
            out_product(2, U_DOWN0, CTF, PAIR_DOWN0, 0, glu_ready(0), lambda j: turn0(CTF - 1) if j == 0 else None)

            def kvq_turn(i, m):
                pe.wait_ge(k_ev, 2 * (0, 2, 3, 5)[i] + m + 1)
                if i == 0:
                    pe.wait_ge(q_gm, 4)
                elif i == 2:
                    pe.wait_ge(k_cp, 2 * i + m)
                elif i == 3:
                    pe.wait_ge(t_on, 7 + m)
                for n in range(4):
                    mm = turn(KQ_BANK[i][m][:, n * P:(n + 1) * P], st[:, m, n * P:(n + 1) * P])
                mm.then_inc(k_tr, 1)

            def kvq_step(j, m0={}, m1={}):
                for m in range(M):
                    if j >= 2:
                        pe.wait_ge(k_ev, 2 * (j - 2) + m + 1)
                    a, b = (yth3, ytl3) if j % 3 == 2 else (xth, xtl)
                    in_group(pair_bank(j + PAIR_KVQ, m)[:, :], m, U_KVQ + 2 * j, a=a, b=b,
                             norm=n_lo if j == 0 else q_lo if j == 2 else None, count=8 if j == 0 else 0,
                             mid=last_turn(2) if j == 0 and m == 0 else None, hooks=m1 if m else m0)

            def heads(h0, n, q, kk, sb, pt, v, s_banks, p_banks, o_banks, shared=False):
                def scores(i):
                    h = h0 + i
                    if i >= 2:
                        pe.wait_ge(t_on if shared else t_sb, h - 1)
                    p, c = slice(DH * (i % 2), DH * (i % 2) + DH), i // 2
                    pe.matmul(s_banks[i % 2][:, 0:P], q[p, c, 0:P], kk[p, c, 0:P], start=True, stop=True)
                    pe.matmul(s_banks[i % 2][:, P:3 * P], q[p, c, P:2 * P], kk[p, c, :], start=True,
                              stop=True).then_inc(t_s, 1)

                def p_turn(i):
                    h = h0 + i
                    pe.wait_ge(t_p, 2 * h + 2)
                    if i >= 2 or (i and p_banks[0] is p_banks[1]):
                        pe.wait_ge(t_ptc, h if p_banks[0] is p_banks[1] else h - 1)
                    for n3 in range(3):
                        mm = turn(p_banks[i % 2][:, n3 * P:(n3 + 1) * P], sb[:, i % 2, n3 * P:(n3 + 1) * P])
                    mm.then_inc(t_pt, 1)

                def pv(i):
                    h = h0 + i
                    pe.wait_ge(t_ptc, h + 1)
                    if i >= 2:
                        pe.wait_ge(t_on, h - 1)
                    o = o_banks[i % 2]
                    pe.matmul(o[:, 0:DH], pt[:, i % 2, 0:P], v(0, i), start=True, stop=True)
                    pe.matmul(o[:, DH:2 * DH], pt[:, i % 2, P:2 * P], v(0, i), start=True, stop=False)
                    pe.matmul(o[:, DH:2 * DH], pt[:, i % 2, 2 * P:3 * P], v(1, i), start=False,
                              stop=True).then_inc(t_o, 1)

                return scores, p_turn, pv

            h_s, h_t, h_v = heads(0, HEADS, qT, kT, sb1, pt1, lambda m, i: vt[:, m, DH * i:DH * i + DH],
                                  tb[0:2], [tb[2], tb[2]], [tb[0][:, 384:512], tb[1][:, 384:512]], shared=True)

            def beside(p):
                def run():
                    i = p // 2
                    if p == 0:
                        pe.wait_ge(k_cp, 4)
                    if p % 2 == 0:
                        if i < 8:
                            h_s(i)
                        if 1 <= i <= 8:
                            h_t(i - 1)
                    elif 1 <= i <= 8:
                        h_v(i - 1)
                    if p in (5, 7):
                        kvq_turn(2, (p - 5) // 2)
                return run

            kvq_step(0)
            kvq_step(1, m0={7: lambda: (kvq_turn(0, 0), kvq_turn(0, 1))})
            kvq_step(2)
            kvq_step(3, m0={7: lambda: (kvq_turn(1, 0), kvq_turn(1, 1))}, m1={3: beside(0), 5: beside(1), 7: beside(2)})
            for j in (4, 5):
                kvq_step(j, *({kt: beside(8 * j - 29 + 4 * m + kt // 2) for kt in (1, 3, 5, 7)} for m in range(M)))

            qTo = qT[:, :, :].rearrange("p c (m d) -> p c m d", d=P)

            def y_turn(b):
                m, c = b % 2, b // 2
                pe.wait_ge(t_on, 8 * c + 8)
                for i in range(4):
                    mm = turn(tb[2 + m][:, i * P:(i + 1) * P], qTo[:, 4 * c + i, m, :])
                mm.then_inc(w_tr, 1)

            y_turn(0)
            y_turn(1)
            kvq_turn(3, 0)
            kvq_turn(3, 1)
            pe.wait_ge(k_cp, 8)
            h_s(8)

            def wo_ready(j):
                if isinstance(j, tuple):
                    pe.wait_ge(k_ev, 12)
                elif j % 2 == 0:
                    pe.wait_ge(w_lo, 2 * (j // 2) + 2)

            def beside_out(i):
                def run():
                    if i > 8:
                        h_v(i - 1)
                    h_t(i)
                    if i + 1 < HEADS:
                        h_s(i + 1)
                    if i == HEADS - 1:
                        h_v(i)
                        y_turn(2)
                        y_turn(3)
                return run

            out_product(3, U_WO, 4, PAIR_WO, 8, wo_ready, hooks={(i // 4, i % 4): beside_out(8 + i) for i in range(8)})
            turn1 = glu(1, U_GLU1, 3, PAIR_GLU1)
            out_product(4, U_DOWN1, CTF, PAIR_DOWN1, 0, glu_ready(1), lambda j: turn1(CTF - 1) if j == 0 else None)
            for q in range(2):
                norm_turn(4, q, f_app, 1)

            for l in range(2):
                U0, k = gu(l), 4 + 2 * l
                pair = pair_mix(l)

                def step(j, m0={}, m1={}, end=None):
                    for m in range(M):
                        if j >= 2:
                            if j == 2:
                                pe.wait_ge(x_gated, 2 * l + m + 1)
                            else:
                                pe.wait_ge(x_ev, 10 * l + 2 * (j - 3) + m + 1)
                        in_group(pair_bank(j + pair, m)[:, :], m, U0 + MIX_END[j] - 2, norm=n_lo if j == 0 else None,
                                 count=4 * k, mid=last_turn(k) if j == 0 and m == 0 and l else None,
                                 hooks=m1 if m else m0)
                        if m == 0 and end is not None:
                            end()

                def second_turns():
                    norm_turn(4, 2, f_app, 2)
                    norm_turn(4, 3)

                step(0, m0={3: second_turns} if l == 0 else {})
                pe.wait_ge(x_gl, l + 1)
                for m in range(M):
                    for kt in range(KT):
                        ts, ws = slice(m * P, (m + 1) * P), slice(RANK * kt, RANK * kt + RANK)
                        mm = split3(tb[0][:, RANK * m:RANK * m + RANK], xth[:, kt, ts], xtl[:, kt, ts], ginh[:, ws],
                                    ginl[:, ws], kt == 0, kt == KT - 1)
                mm.then_inc(x_g16, 1)

                def conv_turn():
                    for m in range(M):
                        pe.wait_ge(x_gated, 2 * l + m + 1)
                        for a in range(2):
                            mm = turn(tb[1][:, a * SEQ + m * P:a * SEQ + (m + 1) * P], hc[:, m, a * P:(a + 1) * P])
                    mm.then_inc(x_ctr, 1)

                def gate_turn():
                    pe.wait_ge(x_g16c, 2 * l + 2)
                    for m in range(M):
                        mm = turn(tb[2][0:RANK, m * P:(m + 1) * P], g16[:, m, :])
                    mm.then_inc(x_gT, 1)

                def qk_turn():
                    pe.wait_ge(x_ev, 10 * l + 2)
                    pe.wait_ge(x_cpad, l + 1)
                    for z in range(2):
                        for a in range(2):
                            for m in range(M):
                                mm = turn(tb[1 + z][:, a * SEQ + m * P:a * SEQ + (m + 1) * P],
                                          gqk[:, m, 256 * z + a * P:256 * z + (a + 1) * P])
                        mm.then_inc(x_qktr, 1)

                def logits():
                    pe.wait_ge(x_gTc, l + 1)
                    for m in range(M):
                        o = tb[3][:, 256 * m:256 * m + 256]
                        pe.matmul(o, gT[0:RANK, m * P:(m + 1) * P], gw_sb[0:RANK, :], start=True, stop=False)
                        mm = pe.matmul(o, ones[0:1, :], gb_sb[0:1, :], start=False, stop=True)
                    mm.then_inc(x_lg, 1)

                def cumsum():
                    pe.wait_ge(x_la, l + 1)
                    for a in range(2):
                        for m in range(M):
                            mm = pe.matmul(tb[3][:, a * SEQ + m * P:a * SEQ + (m + 1) * P], la[:, m, a * P:(a + 1) * P],
                                           tri[:, :], start=True, stop=True)
                    mm.then_inc(x_cs, 1)

                def kd_turn():
                    pe.wait_ge(x_kd, l + 1)
                    for m in range(M):
                        for a in range(2):
                            mm = turn(tb[0][:, m * 256 + a * P:m * 256 + (a + 1) * P], dG[:, a, m * P:(m + 1) * P])
                    mm.then_inc(x_kdtr, 1)

                def gla_scores(b):
                    p = slice(DK * b, DK * b + DK)
                    for m in range(M):
                        for a in range(2):
                            c = (2 * m + a) * P
                            mm = pe.matmul(tb[1 + b][:, c:c + P], nG[p, a, m * P:(m + 1) * P],
                                           eG[p, a, m * P:(m + 1) * P], start=True, stop=True)
                    mm.then_inc(x_A, 1)

                def state_inc(n):
                    m, p = n // 4, slice(GCH * (n % 4), GCH * (n % 4) + GCH)
                    if n == 0:
                        pe.wait_ge(x_kdc, l + 1)
                        pe.wait_ge(x_ev, 10 * l + 4)
                    if n >= 2:
                        pe.wait_ge(x_St, (NCH - 1) * l + n - 1)
                    for a in range(2):
                        for b in range(2):
                            h = 2 * a + b
                            mm = pe.matmul(tb[3 * (n % 2)][DK * b:DK * b + DK, P * a:P * a + P],
                                           kdt[p, m, h * DK:(h + 1) * DK], gv[p, m, h * DV:(h + 1) * DV],
                                           start=True, stop=True)
                    mm.then_inc(x_dS, 1)

                def mqk_turn():
                    pe.wait_ge(x_ev, 10 * l + 6)
                    pe.wait_ge(x_Am, 2 * l + 2)
                    for z in range(2):
                        for a in range(2):
                            for m in range(M):
                                mm = turn(tb[1 + z][:, a * SEQ + m * P:a * SEQ + (m + 1) * P],
                                          mqk[:, m, 256 * z + a * P:256 * z + (a + 1) * P])
                        mm.then_inc(x_mtr, 1)

                def gla_out(b):
                    if b == 0:
                        pe.wait_ge(x_St, (NCH - 1) * (l + 1))
                    else:
                        pe.wait_ge(x_oc, 2 * l + 1)
                    p = slice(DK * b, DK * b + DK)
                    for m in range(M):
                        for a in range(2):
                            h, c0 = 2 * a + b, (2 * m + a) * P
                            mm = pe.matmul(tb[0][:, c0:c0 + P], aT[:, b, c0:c0 + P], gv[:, m, h * DV:(h + 1) * DV],
                                           start=True, stop=False, skip_group_check=True)
                            for c in range(4):
                                n = 4 * m + c
                                if n == 0:
                                    continue
                                mm = pe.matmul(tb[0][GCH * c:GCH * (c + 1), c0:c0 + P],
                                               eG[p, a, n * GCH:(n + 1) * GCH], st_g[p, n - 1, a, :], start=False,
                                               stop=True, skip_group_check=True)
                    mm.then_inc(x_o, 1)

                def ln_turn():
                    pe.wait_ge(x_St, (NCH - 1) * l + 6)
                    pe.wait_ge(x_tap, TAPS * (l + 1))
                    pe.wait_ge(x_tap1, (TAPS - POOL_TAPS + 1) * (l + 1))
                    for m in range(M):
                        for a in range(2):
                            mm = turn(tb[3][:, m * 256 + a * P:m * 256 + (a + 1) * P], cacc[:, a, m * P:(m + 1) * P])
                    mm.then_inc(x_ltr, 1)

                def ln_back():
                    pe.wait_ge(x_nrm, 2 * l + 2)
                    for a in range(2):
                        for m in range(M):
                            mm = turn(tb[3][:, a * SEQ + m * P:a * SEQ + (m + 1) * P], cvn[:, m, a * P:(a + 1) * P])
                    mm.then_inc(x_btr, 1)

                def y_turn(m):
                    pe.wait_ge(x_on2, 2 * l + m + 1)
                    if m:
                        pe.wait_ge(x_yg, 3 * l + 1)
                    for i in range(4):
                        mm = turn(tb[0][:, i * P:(i + 1) * P], og[:, m, i * P:(i + 1) * P])
                    mm.then_inc(x_ytr, 1)

                def mo_turn():
                    pe.wait_ge(x_on, l + 1)
                    pe.wait_ge(x_yg, 3 * l + 2)
                    for a in range(2):
                        for m in range(M):
                            mm = turn(tb[0][:, a * SEQ + m * P:a * SEQ + (m + 1) * P], mo[:, m, a * P:(a + 1) * P])
                    mm.then_inc(x_ytr, 1)

                h_s, h_t, h_v = heads(HEADS + 4 * l, 4, mqT, mkT, sb2, pt2, lambda m, i: mv[:, m, DH * i:DH * i + DH],
                                      tb[2:4], [tb[1], tb[1]], [tb[2][:, 384:512], tb[3][:, 384:512]], shared=True)

                def all_of(*parts):
                    def run():
                        for f, a in parts:
                            f(*a)
                    return run

                step(1, m0={3: gate_turn}, end=conv_turn, m1={3: logits})
                step(2, end=cumsum, m1={3: qk_turn})
                step(3, m0={5: kd_turn}, end=all_of((gla_scores, (0,)), (gla_scores, (1,))),
                     m1={5: lambda: state_inc(0)})
                state_inc(1)
                s = (U0 + 8) % SLOTS
                pe.wait_ge(lo_ready, U0 + 9)
                for m in range(M):
                    pe.wait_ge(x_ev, 10 * l + 2 + m + 1)
                    for kt in range(KT):
                        ts, ws = slice(m * P, (m + 1) * P), slice(256 * kt, 256 * kt + 256)
                        mm = split3(pair_bank(4 + pair, m)[:, 0:256], xth[:, kt, ts], xtl[:, kt, ts], whi[:, s, ws],
                                    wlo[:, s, ws], kt == 0, kt == KT - 1)
                        if m == 0 and kt == 3:
                            state_inc(2)
                    mm.then_inc(m0_done if m == 0 else unit_used, 1)
                    if m == 0:
                        mqk_turn()
                        state_inc(3)
                state_inc(4)

                def first_scores():
                    pe.wait_ge(x_mcp, 2 * l + 2)
                    h_s(0)

                def second_scores():
                    pe.wait_ge(x_sl, 2 * l + 2)
                    h_s(1)

                def first_pv():
                    pe.wait_ge(x_ev, 10 * l + 8)
                    h_v(0)

                step(5, m0={1: lambda: state_inc(5), 3: all_of((state_inc, (6,)), (first_scores, ())),
                            5: all_of((ln_turn, ()), (gla_out, (0,)))},
                     end=lambda: h_t(0),
                     m1={1: all_of((gla_out, (1,)), (ln_back, ())), 5: all_of((first_pv, ()), (second_scores, ()))})
                h_s(2)

                def mix_ready(j):
                    if isinstance(j, tuple):
                        pe.wait_ge(x_ev, 10 * l + (8 if j[1] == 0 else 10))
                    else:
                        pe.wait_ge(x_yl, 4 * l + (1, 2, 3, 4)[j])

                out_product(k + 1, U0 + 11, 4, pair, 0, mix_ready, order=MIX_ORDER, hooks={
                    (0, 0): lambda: h_t(1), (0, 1): all_of((h_v, (1,)), (y_turn, (0,))), (0, 2): lambda: y_turn(1),
                    (0, 3): all_of((h_s, (3,)), (h_t, (2,))), (1, 0): lambda: h_v(2),
                    (1, 1): all_of((pe.wait_ge, (x_yl, 4 * l + 3)), (h_t, (3,))), (1, 2): lambda: h_v(3),
                    (2, 2): mo_turn})

                U1 = U0 + 15

                def ffn_turn(j, t=0):
                    pe.wait_ge(f_ev, 2 * CTF * l + 2 * j + 2 + 4 * t)
                    if j >= 2:
                        pe.wait_ge(f_t2, CTF * l + j - 1 + 2 * t)
                    for a in range(4):
                        for m in range(M):
                            mm = turn(tb[2 * (j % 2) + a // 2][:, (a % 2) * SEQ + m * P:(a % 2) * SEQ + (m + 1) * P],
                                      us[:, j % 2, m, a * P:(a + 1) * P])
                    mm.then_inc(f_tr, 1)

                def fstep(j, t=0):
                    for m in range(M):
                        if j >= 2:
                            pe.wait_ge(f_ev, 2 * CTF * l + 2 * (j - 2) + m + 1 + 4 * t)
                        in_group(pair_bank(j + pair, m)[:, :], m, U1 + 2 * j, t, norm=n_lo if j == 0 else None,
                                 count=4 * (k + 1), mid=last_turn(k + 1) if j == 0 and m == 0 else None)
                        if m == 0 and j >= 1:
                            ffn_turn(j - 1, t)

                for j in range(3):
                    fstep(j)
                with pe.Fori(0, (CTF - 3) // 2) as t:
                    fstep(3, t)
                    fstep(4, t)

                def ffn_ready(j):
                    if isinstance(j, tuple):
                        pe.wait_ge(f_ev, 2 * CTF * l + 2 * CTF - 2 * (1 - j[1]))
                    else:
                        pe.wait_ge(f_lo, CTF * l + j + 1)

                out_product(k + 2, U1 + 2 * CTF, CTF, pair_fdown(l), 0, ffn_ready,
                            lambda j: ffn_turn(CTF - 1) if j == 0 else None)


def _in_units(w, parts):
    units = []
    for cols in parts:
        block = np.concatenate([w[:, a:a + n] for a, n in cols], axis=1).reshape(KT, P, -1)
        if block.shape[2] == 512:
            for half in range(2):
                units.append(block[4 * half:4 * half + 4].transpose(1, 0, 2).reshape(P, UNIT))
        else:
            units.append(block.transpose(1, 0, 2).reshape(P, UNIT))
    return units


def _out_units(w):
    return list(w.reshape(-1, 2, P, D).transpose(0, 2, 1, 3).reshape(-1, P, UNIT))


def _gate_up(n):
    return [[(256 * j, 256), (HID + 256 * j, 256)] for j in range(n)]


def _tiles(v):
    v = v.reshape(v.shape[:-1] + (-1, P))
    return np.ascontiguousarray(np.moveaxis(v, -1, 0))


def kernel(x, a_norm, a_w_in, a_sgu_norm, a_w_spatial, a_b_spatial, a_w_out, kv_norm, w_kv, b_norm, b_w_q,
           b_rel_bias, b_w_o, ffn_norm, ffn_w_gate_up, ffn_w_down, final_norm, norm_mix_g_2, w_in_2, conv_w_2,
           conv_b_2, conv_ln_g_2, conv_ln_b_2, moba_out_g_2, gla_gate_w_2, gla_gate_b_2, gla_out_g_2, w_out_2,
           norm_ffn_g_2, ffn_w_up_2, ffn_conv_w_2, ffn_conv_b_2, ffn_w_down_2, final_g_2):
    import concourse.bacc as bacc
    from concourse.bass_utils import run_bass_kernel_spmd

    A = np.asarray
    units = _in_units(A(a_w_in)[0], [[(512 * j, 512)] for j in (4, 5, 6, 7, 0, 1, 2, 3)])
    units += _out_units(A(a_w_out)[0])
    units += _in_units(A(ffn_w_gate_up)[0], _gate_up(CTF)) + _out_units(A(ffn_w_down)[0])
    for j in range(2):
        units += _in_units(A(w_kv), [[(512 * j, 512)], [(D + 512 * j, 512)]])
        units += _in_units(A(b_w_q)[0], [[(512 * j, 512)]])
    units += _out_units(A(b_w_o)[0])
    units += _in_units(A(ffn_w_gate_up)[1], _gate_up(CTF)) + _out_units(A(ffn_w_down)[1])
    mix = [[(0, 512)], [(1280, 512)], [(1792, 512)], [(512, 512)], [(1024, 256)], [(2320, 512)]]
    for l in range(2):
        w_out = _out_units(A(w_out_2)[l])
        units += _in_units(A(w_in_2)[l], mix) + [w_out[i] for i in MIX_ORDER]
        units += _in_units(A(ffn_w_up_2)[l], _gate_up(CTF)) + _out_units(A(ffn_w_down_2)[l])
    assert len(units) == TOTAL
    gains = [A(a_norm)[0], A(ffn_norm)[0], A(kv_norm), A(ffn_norm)[1], A(norm_mix_g_2)[0], A(norm_ffn_g_2)[0],
             A(norm_mix_g_2)[1], A(b_norm)[0], A(norm_ffn_g_2)[1]]
    fw, fb = A(ffn_conv_w_2), A(ffn_conv_b_2)
    taps = np.concatenate([fw, fb[:, None, :]], axis=1)
    taps = taps.reshape(2, 4, 2, CTF, 2, P).transpose(5, 0, 3, 2, 4, 1).reshape(P, 2, CTF * 16)
    cw = np.concatenate([A(conv_w_2), A(conv_b_2)[:, None, :]], axis=1)
    arrays = {
        "x_in": A(x)[0],
        "stream": np.stack(units),
        "cols": _tiles(np.stack(gains)),
        "bs_col": A(a_b_spatial)[0].T,
        "ws_t": A(a_w_spatial)[0].transpose(2, 0, 1),
        "gs_row": A(a_sgu_norm),
        "fin_row": A(final_norm)[None],
        "fin2_row": A(final_g_2)[None],
        "rel_rows": A(b_rel_bias)[0][:, MAX_REL + P + np.arange(P)[:, None] - np.arange(SEQ)[None, :]].transpose(1, 0, 2),
        "ffn_cw": taps,
        "conv_w": cw.reshape(2, 32, 2, P).transpose(3, 0, 2, 1),
        "conv_ln": np.stack([A(conv_ln_g_2), A(conv_ln_b_2)]).reshape(2, 2, 2, P).transpose(3, 1, 2, 0),
        "moba_g": _tiles(A(moba_out_g_2)),
        "gla_g": _tiles(A(gla_out_g_2)),
        "gate_w": A(gla_gate_w_2),
        "gate_b": A(gla_gate_b_2)[:, None, :],
        "gate_in": A(w_in_2)[:, :, 2304:2320].reshape(2, KT, P, RANK).transpose(0, 2, 1, 3).reshape(2, P, KT * RANK),
    }
    nc = bacc.Bacc("TRN2", target_bir_lowering=False, num_devices=1)
    sent, args = {}, {}
    for name, a in arrays.items():
        a = np.ascontiguousarray(a)
        sent["in_" + name] = a
        args[name] = nc.dram_tensor("in_" + name, a.shape, mybir.dt.from_np(a.dtype), kind="ExternalInput").ap()
    out = nc.dram_tensor("out_0", (SEQ, D), F32, kind="ExternalOutput").ap()
    two_blocks_kernel(nc, out=out, **args)
    r = run_bass_kernel_spmd(nc, [sent], core_ids=[0])
    return np.asarray(r.results[0]["out_0"]).reshape(1, SEQ, D)
```
